# Optimizing a Trainium2 kernel written in Bass

```python
import math
import jax, jax.numpy as jnp
from jax import lax
import numpy as np

D_MODEL = 1024
BATCH = 1
SEQ = 2048
DEPTH = 1

CHUNK = 64
Q_BLOCK = 128
N_MEM = 256
EPS = 1e-6
ROPE_THETA = 500000.0

SB_HEADS = 8
SB_HEAD_DIM = D_MODEL // 16
SB_WIDTH = SB_HEADS * SB_HEAD_DIM
DF_HEADS = 4
DF_QK_DIM = D_MODEL // 32
DF_V_DIM = 2 * DF_QK_DIM
DF_WIDTH = DF_HEADS * DF_V_DIM
DF_ROT_DIMS = DF_QK_DIM // 4
MEM_HEADS = 4
MEM_HEAD_DIM = D_MODEL // 16
MEM_WIDTH = MEM_HEADS * MEM_HEAD_DIM
MIX_WIDTH = SB_WIDTH + DF_WIDTH + MEM_WIDTH

PROJ_SIZES = (SB_WIDTH, SB_WIDTH, SB_WIDTH, SB_WIDTH,
              2 * DF_HEADS * DF_QK_DIM, 2 * DF_HEADS * DF_QK_DIM,
              DF_WIDTH, DF_WIDTH,
              MEM_WIDTH, MEM_WIDTH)
PROJ_WIDTH = sum(PROJ_SIZES)

kernel_name = 'hymba_stickbreak_diffattn_memxattn_block'

def _rmsnorm(x, g):
    xf = x.astype(jnp.float32)
    y = xf * lax.rsqrt(jnp.mean(xf * xf, axis=-1, keepdims=True) + EPS)
    return (y * g.astype(jnp.float32)).astype(x.dtype)

def _split_proj(p):
    parts, off = [], 0
    for n in PROJ_SIZES:
        parts.append(p[..., off:off + n])
        off += n
    return parts

def _partial_rope(x, cos, sin):
    half = DF_ROT_DIMS // 2
    x1 = x[..., :half]
    x2 = x[..., half:DF_ROT_DIMS]
    r1 = (x1 * cos - x2 * sin).astype(x.dtype)
    r2 = (x2 * cos + x1 * sin).astype(x.dtype)
    return jnp.concatenate([r1, r2, x[..., DF_ROT_DIMS:]], axis=-1)

def _to_blocks(a):
    b, s = a.shape[:2]
    a = a.reshape((b, s // Q_BLOCK, Q_BLOCK) + a.shape[2:])
    return jnp.moveaxis(a, 1, 0)

def _from_blocks(a):
    a = jnp.moveaxis(a, 0, 1)
    return a.reshape((a.shape[0], a.shape[1] * a.shape[2]) + a.shape[3:])

def _stick_breaking(q, k, v):
    s_len = q.shape[1]
    scale = SB_HEAD_DIM ** -0.5
    key_idx = jnp.arange(s_len)

    def block(args):
        qb, t0 = args
        z = jnp.einsum('bqhd,bkhd->bhqk', qb, k).astype(jnp.float32) * scale
        q_idx = t0 + jnp.arange(Q_BLOCK)
        strict = key_idx[None, :] < q_idx[:, None]
        log_1mb = jnp.where(strict, jax.nn.log_sigmoid(-z), 0.0)
        between = lax.cumsum(log_1mb, axis=3, reverse=True) - log_1mb
        w = jnp.where(strict, jnp.exp(jax.nn.log_sigmoid(z) + between), 0.0)
        return jnp.einsum('bhqk,bkhd->bqhd', w.astype(v.dtype), v)

    starts = jnp.arange(s_len // Q_BLOCK, dtype=jnp.int32) * Q_BLOCK
    return _from_blocks(lax.map(block, (_to_blocks(q), starts)))

def _diff_attention(q, k, v, lam, lambda_init, g_subln):
    s_len = q.shape[1]
    scale = DF_QK_DIM ** -0.5
    key_chunk = jnp.arange(s_len) // CHUNK

    def block(args):
        qb, t0 = args
        sc = jnp.einsum('bqhmd,bkhmd->bhmqk', qb, k).astype(jnp.float32) * scale
        q_chunk = (t0 + jnp.arange(Q_BLOCK)) // CHUNK
        allowed = key_chunk[None, :] <= q_chunk[:, None]
        p = jax.nn.softmax(jnp.where(allowed, sc, -jnp.inf), axis=-1)
        a = p[:, :, 0] - lam * p[:, :, 1]
        return jnp.einsum('bhqk,bkhe->bqhe', a.astype(v.dtype), v)

    starts = jnp.arange(s_len // Q_BLOCK, dtype=jnp.int32) * Q_BLOCK
    o = _from_blocks(lax.map(block, (_to_blocks(q), starts)))
    return _rmsnorm(o, g_subln) * (1.0 - lambda_init)

def setup_inputs(seed: int = 0) -> dict:
    key = jax.random.key(seed)
    ks = jax.random.split(key, 12)
    f32 = jnp.float32
    x = jax.random.normal(ks[0], (BATCH, SEQ, D_MODEL), f32)
    mem = jax.random.normal(ks[1], (BATCH, N_MEM, D_MODEL), f32)
    offset = jax.random.randint(ks[2], (BATCH, 1), 0, 4096, dtype=jnp.int32)
    positions = (offset + jnp.arange(SEQ, dtype=jnp.int32)[None, :]).astype(jnp.int32)
    w_in = jax.random.normal(ks[3], (DEPTH, D_MODEL, PROJ_WIDTH), f32) * D_MODEL ** -0.5
    w_mem_kv = jax.random.normal(ks[4], (DEPTH, D_MODEL, 2 * MEM_WIDTH), f32) * D_MODEL ** -0.5
    w_out = jax.random.normal(ks[5], (DEPTH, MIX_WIDTH, D_MODEL), f32) * MIX_WIDTH ** -0.5
    g_pre = 1.0 + 0.02 * jax.random.normal(ks[6], (DEPTH, D_MODEL), f32)
    g_post = 1.0 + 0.02 * jax.random.normal(ks[7], (DEPTH, D_MODEL), f32)
    g_mem = 1.0 + 0.02 * jax.random.normal(ks[8], (DEPTH, D_MODEL), f32)
    g_subln = 1.0 + 0.02 * jax.random.normal(ks[9], (DEPTH, DF_V_DIM), f32)
    df_lambda = 0.1 * jax.random.normal(ks[10], (DEPTH, 4, DF_QK_DIM), f32)
    return {'x': x, 'mem': mem, 'positions': positions, 'w_in': w_in, 'w_mem_kv': w_mem_kv,
            'w_out': w_out, 'g_pre': g_pre, 'g_post': g_post, 'g_mem': g_mem,
            'g_subln': g_subln, 'df_lambda': df_lambda}

def reference(x, mem, positions, w_in, w_mem_kv, w_out, g_pre, g_post, g_mem, g_subln, df_lambda):
    b, s_len, _ = x.shape
    n_mem = mem.shape[1]
    inv_freq = 1.0 / (ROPE_THETA ** (jnp.arange(0, DF_ROT_DIMS, 2, dtype=jnp.float32) / DF_ROT_DIMS))
    ang = positions.astype(jnp.float32)[:, :, None] * inv_freq
    cos = jnp.cos(ang)[:, :, None, None, :]
    sin = jnp.sin(ang)[:, :, None, None, :]

    for layer in range(DEPTH):
        lambda_init = 0.8 - 0.6 * math.exp(-0.3 * layer)
        h = _rmsnorm(x, g_pre[layer])
        proj = h @ w_in[layer]
        sb_q, sb_k, sb_v, sb_g, df_q, df_k, df_v, df_g, m_q, m_g = _split_proj(proj)

        shp = (b, s_len, SB_HEADS, SB_HEAD_DIM)
        y_sb = _stick_breaking(sb_q.reshape(shp), sb_k.reshape(shp), sb_v.reshape(shp))
        y_sb = y_sb.reshape(b, s_len, SB_WIDTH) * jax.nn.silu(sb_g)

        qk_shp = (b, s_len, DF_HEADS, 2, DF_QK_DIM)
        dq = _partial_rope(df_q.reshape(qk_shp), cos, sin)
        dk = _partial_rope(df_k.reshape(qk_shp), cos, sin)
        lp = df_lambda[layer].astype(jnp.float32)
        lam = jnp.exp(jnp.sum(lp[0] * lp[1])) - jnp.exp(jnp.sum(lp[2] * lp[3])) + lambda_init
        y_df = _diff_attention(dq, dk, df_v.reshape(b, s_len, DF_HEADS, DF_V_DIM),
                               lam, lambda_init, g_subln[layer])
        y_df = y_df.reshape(b, s_len, DF_WIDTH) * jax.nn.silu(df_g)

        mkv = (_rmsnorm(mem, g_mem[layer]) @ w_mem_kv[layer]).reshape(b, n_mem, 2, MEM_HEADS, MEM_HEAD_DIM)
        mq = m_q.reshape(b, s_len, MEM_HEADS, MEM_HEAD_DIM)
        sc = jnp.einsum('bshd,bmhd->bhsm', mq, mkv[:, :, 0]).astype(jnp.float32) * MEM_HEAD_DIM ** -0.5
        pm = jax.nn.softmax(sc, axis=-1).astype(mkv.dtype)
        y_m = jnp.einsum('bhsm,bmhd->bshd', pm, mkv[:, :, 1]).reshape(b, s_len, MEM_WIDTH) * jax.nn.silu(m_g)

        y = jnp.concatenate([y_sb, y_df, y_m], axis=-1) @ w_out[layer]
        x = x + _rmsnorm(y, g_post[layer])
    return x


_drawn_inputs = setup_inputs


def setup_inputs(seed=0):
    import zlib

    import numpy as np

    out = dict(_drawn_inputs(seed))
    spreads = {}
    factors = {'g_post': 4.056, 'g_mem': 8.0, 'g_subln': 5.688, 'df_lambda': 4.744}
    for name, (base, spread) in spreads.items():
        noise = np.random.default_rng([zlib.crc32(name.encode()), seed]).standard_normal(out[name].shape)
        drawn = base * np.exp(spread * noise) if base else spread * noise
        out[name] = __import__('jax').numpy.asarray(drawn.astype(out[name].dtype))
    for name, factor in factors.items():
        out[name] = (out[name] * factor).astype(out[name].dtype)
    return out
```

```python
from contextlib import ExitStack
import math

import numpy as np
import concourse.bass as bass
from concourse import mybir

F32 = mybir.dt.float32
F32R = mybir.dt.float32r
BF16 = mybir.dt.bfloat16
I32 = mybir.dt.int32
ACT = mybir.ActivationFunctionType
ALU = mybir.AluOpType
AXX = mybir.AxisListType.X

P = 128
D = 1024
S = 2048
DC = D // P
SB = S // P
TQ = 512
NT = S // TQ
NMEM = 256
EPS = 1e-6
HD = 64
SB_H, DF_H, M_H = 8, 4, 4
DQ = 32
V_W = (SB_H + DF_H) * HD
WIDE, NARROW = 256, 128
N_V, N_G = V_W // WIDE, D // WIDE
C_SB = N_V + N_G
C_MK = C_SB + SB_H
C_M = C_MK + 4
C_DF = C_M + M_H // 2
NEG = -1e30
E_MAX = 1e13
THETA = 500000.0
LAMBDA_INIT = 0.8 - 0.6 * math.exp(-0.3 * 0)

SB_STEPS = [(t, kb, max(0, kb - 4 * t)) for t in range(NT) for kb in range(4 * t + 4)]
N_ST = len(SB_STEPS)
SB_LAST = {t: max(i for i, s in enumerate(SB_STEPS) if s[0] == t) for t in range(NT)}
SB_MULS = [i for i, s in enumerate(SB_STEPS) if s[1] > 0]

DF_STEPS = [(t, kb, max(0, kb - 4 * t), m) for t in range(NT) for kb in range(4 * t + 4) for m in range(2)]
N_DF = len(DF_STEPS)
DF_UNITS = []
for _t in range(NT):
    DF_UNITS += [("max", _t, j, m, c, min(TQ, (4 * _t + j + 1) * P - c * TQ))
                 for j in range(4) for m in range(2) for c in range(_t + 1)]
    DF_UNITS += [("row", _t, 0, m, 0, 0) for m in range(2)]
N_UN = len(DF_UNITS)


def df_unit_range(t):
    idx = [u for u, x in enumerate(DF_UNITS) if x[1] == t]
    return idx[0], idx[-1] + 1


def df_order(final):
    out = [("u", u) for u in range(*df_unit_range(0))]
    step = 0
    for t in range(NT):
        n = 8 * (t + 1)
        units = list(range(*df_unit_range(t + 1))) if t + 1 < NT else []
        body, rows = units[:-2], units[-2:]
        room = max(n - 4, 1)
        for k in range(n):
            out.append(("s", step))
            take = -(-len(body) // max(room - k, 1)) if body else 0
            out += [("u", body.pop(0)) for _ in range(min(take, len(body)))]
            if k == n - 2:
                out += [("u", r) for r in rows]
            if step:
                out.append(("p", step - 1))
            if t:
                out += [(e, t - 1) for e, at in (("f", 1), ("l", 3), ("g", 5)) if k == at]
            if final and t == NT - 1 and k >= 8 and k % 3 == 2:
                out.append(("w", (k - 8) // 3))
            step += 1
    return out + [("p", step - 1), ("f", NT - 1), ("l", NT - 1), ("g", NT - 1)]


DF_ORDER = {final: df_order(final) for final in (False, True)}


def build(nc, x, mem, positions, w_wide, w_narrow, w_out, g_pre, g_post, g_mem, g_subln,
          df_lambda, const_sq, const_col, out):
    ctx = ExitStack()
    with ctx:
        def sb(name, shape, dt, stack=ctx):
            return stack.enter_context(nc.sbuf_tensor(name, shape, dt))

        def sem(name):
            return ctx.enter_context(nc.semaphore(name))

        def dram(name, shape):
            return nc.dram_tensor(name, shape, F32, kind="Internal").ap()

        v_scr = dram("v_scr", (SB_H + DF_H, S, HD))
        gate_scr = dram("gate_scr", (S, D))
        y_scr = dram("y_scr", (S, D))
        rot_scr = dram("rot_scr", (2, P, S))

        ident = sb("ident", [P, P], F32)
        negtri = sb("negtri", [P, P], F32)
        rotperm = sb("rotperm", [P, P], F32)
        ident_b = sb("ident_b", [P, P], BF16)
        sb_mask = sb("sb_mask", [P, P], BF16)
        df_mask_kq = sb("df_mask_kq", [P, P], BF16)
        df_mask_qk = sb("df_mask_qk", [P, P], BF16)
        small = sb("small", [P, 256], F32)
        invf = small[:, 0:1]
        lam = small[:, 1:2]
        ident_r = sb("ident_r", [P, P], F32R)
        w_raw = sb("w_raw", [P, DC * WIDE], F32)
        w_hl = sb("w_hl", [P, 2 * DC * WIDE], F32R)
        ring = sb("ring", [P, 6, TQ], F32)
        v1 = sb("v1", [P, SB, HD + 1], F32)
        acc = sb("acc", [P, 2, 4, HD], F32)
        ps = ctx.enter_context(nc.psum_tensor("ps", [P, 8, 512], F32))

        with ExitStack() as first:
            ht_hi = sb("ht_hi", [P, DC, S], F32R, first)
            ht_lo = sb("ht_lo", [P, DC, S], F32R, first)
            with ExitStack() as a:
                xb = sb("xb", [P, 2, D], F32, a)
                hb = sb("hb", [P, 2, D], F32, a)
                gpre_b = sb("gpre_b", [P, D], F32, a)
                cst = sb("cst", [P, 6, P], F32, a)
            with ExitStack() as a:
                ang = sb("ang", [P, S], F32, a)
                turns = sb("turns", [P, S], F32, a)
                red = sb("red", [P, S], F32, a)
                trig = sb("trig", [P, S], F32, a)
            with ExitStack() as a:
                sb_s = sb("sb_s", [P, S], F32R, a)
                sb_ma = sb("sb_ma", [P, S], F32R, a)
                sb_mb = sb("sb_mb", [P, S], F32R, a)
            with ExitStack() as a:
                km_hi = sb("km_hi", [P, 2, NMEM], F32R, a)
                km_lo = sb("km_lo", [P, 2, NMEM], F32R, a)
                vm = sb("vm", [P, 2, M_H * HD], F32, a)
                with ExitStack() as b:
                    mt_hi = sb("mt_hi", [P, DC, NMEM], F32R, b)
                    mt_lo = sb("mt_lo", [P, DC, NMEM], F32R, b)
                with ExitStack() as b:
                    qm_hi = sb("qm_hi", [P, S], F32R, b)
                    qm_lo = sb("qm_lo", [P, S], F32R, b)
            with ExitStack() as a:
                df_s = [sb(f"df_s{m}", [P, S], F32R, a) for m in range(2)]
                df_m = [sb(f"df_m{m}", [P, S], F32R, a) for m in range(2)]
                nm_win = sb("nm_win", [P, 96 + 8], F32R, a)
        with ExitStack() as last:
            wo_hi = sb("wo_hi", [P, DC, D], F32R, last)
            wo_lo = sb("wo_lo", [P, DC, D], F32R, last)
            yt_hi = sb("yt_hi", [P, 2, DC, P], F32R, last)
            yt_lo = sb("yt_lo", [P, 2, DC, P], F32R, last)
            yb = sb("yb", [P, 2, D], F32, last)
            gb = sb("gb", [P, 2, D], F32, last)
            xr = sb("xr", [P, 2, D], F32, last)
            ob = sb("ob", [P, 2, D], F32, last)
            gpost_b = sb("gpost_b", [P, D], F32, last)

        mem_x, mem_h, mem_g = (ring[:, 2 * i:2 * i + 2, :].rearrange("p a b -> p (a b)") for i in range(3))
        gsub_b = small[:, 64:128]
        lam_in = small[:, 128:256]

        def w_hi(cols, dc):
            return w_hl[:, dc * cols:(dc + 1) * cols]

        def w_lo(cols, dc):
            return w_hl[:, (DC + dc) * cols:(DC + dc + 1) * cols]

        def raw(cols, dc):
            return w_raw[:, dc * cols:(dc + 1) * cols]

        spare = w_hl[:, 2 * DC * NARROW:].rearrange("p (a u n) -> p a u n", a=2, u=2)
        hi_tmp, lo_tmp = spare[:, 0], spare[:, 1]
        cos_c = w_raw[:, DC * NARROW:DC * NARROW + TQ]
        sin_c = w_raw[:, DC * NARROW + TQ:DC * NARROW + 2 * TQ]

        def col(k, u, n=1):
            return small[:, 8 + 8 * k + 4 * u:8 + 8 * k + 4 * u + n]

        const_in, const_ok = sem("const_in"), sem("const_ok")
        x_in = [sem("x_in0"), sem("x_in1")]
        x_sq, x_var, x_ln, x_y0, x_nr, h_rows = (sem(n) for n in ("x_sq", "x_var", "x_ln", "x_y0", "x_nr", "h_rows"))
        ht_ps, ht_hi_ok, ht_lo_ok = sem("ht_ps"), sem("ht_hi_ok"), sem("ht_lo_ok")
        w_raw_in, w_hi_ok, w_lo_ok, w_free = sem("w_raw_in"), sem("w_hi_ok"), sem("w_lo_ok"), sem("w_free")
        vg_ps, vg_ok, vg_e, vg_ch = sem("vg_ps"), sem("vg_ok"), sem("vg_e"), sem("vg_ch")
        vg_out = [sem("vg_out0"), sem("vg_out1")]
        pos_in, trig_ch, trig_val, trig_out = sem("pos_in"), sem("trig_ch"), sem("trig_val"), sem("trig_out")
        sp_ps, sp_act, sp_dve = sem("sp_ps"), sem("sp_act"), sem("sp_dve")
        sb_z, sb_e, sb_clamp, sb_ln, sb_sp, sb_cum, sb_w, sb_o, sb_acc, sb_ch = (
            sem("sb_" + n) for n in ("z", "e", "clamp", "ln", "sp", "cum", "w", "o", "acc", "ch"))
        sb_v, sb_yout = sem("sb_v"), [sem("sb_yout0"), sem("sb_yout1")]
        mm_in, mm_sq, mm_ch, mm_ln, mm_y0, mm_h, mm_ps, mm_hi, mm_lo, mm_kv, mm_ka, mm_kd = (
            sem("mm_" + n) for n in ("in", "sq", "ch", "ln", "y0", "h", "ps", "hi", "lo", "kv", "ka", "kd"))
        m_pj, m_qhi, m_qlo = sem("m_pj"), sem("m_qhi"), sem("m_qlo")
        m_s, m_mx, m_nm, m_p, m_t, m_pt, m_o, m_rc, m_y = (
            sem("m_" + n) for n in ("s", "mx", "nm", "p", "t", "pt", "o", "rc", "y"))
        m_yout = [sem("m_yout0"), sem("m_yout1")]
        df_cs, df_pj, df_x, df_px, df_t1, df_t2, df_x2, df_hi, df_lo = (
            sem("df_" + n) for n in ("cs", "pj", "x", "px", "t1", "t2", "x2", "hi", "lo"))
        df_pl_a, df_pl_d, df_pl_p, df_rows0, df_set = (
            sem("df_" + n) for n in ("pl_a", "pl_d", "pl_p", "rows0", "set"))
        df_ups, df_mx, df_cb, df_nm = (sem("df_" + n) for n in ("ups", "mx", "cb", "nm"))
        df_z, df_e, df_o, df_fin, df_fch, df_var, df_ln, df_y0, df_gch, df_yok, df_v = (
            sem("df_" + n) for n in ("z", "e", "o", "fin", "fch", "var", "ln", "y0", "gch", "yok", "v"))
        df_yout = [sem("df_yout0"), sem("df_yout1")]
        pool_go = sem("pool_go")
        lam_ch, lam_e = sem("lam_ch"), sem("lam_e")
        wo_in, wo_hi_ok, wo_lo_ok, gpost_in = [sem("wo_in0"), sem("wo_in1")], sem("wo_hi_ok"), sem("wo_lo_ok"), sem("gpost_in")
        o_in, o_xr, o_out = ([sem(f"o_{n}{u}") for u in range(2)] for n in ("in", "xr", "out"))
        o_yg, o_tps, o_thi, o_tlo, o_ps, o_sq, o_ch, o_var, o_ln, o_y0, o_nr, o_n, o_fin = (
            sem("o_" + n) for n in ("yg", "tps", "thi", "tlo", "ps", "sq", "ch", "var", "ln", "y0", "nr", "n", "fin"))

        block = ctx.enter_context(nc.Block())

        y_rows = y_scr.rearrange("(t j p) n -> t p j n", j=4, p=P)
        v_rows = v_scr.rearrange("h (b p) d -> h p b d", p=P)
        w_raw_n = w_raw[:, 0:DC * NARROW]

        @block.sync
        def _(sp):
            for one in (ht_ps, *vg_out, sb_o, sb_acc, *sb_yout, df_t1, df_t2, df_o, df_mx, df_fin, *df_yout, df_pl_p):
                sp.sem_inc(one, 1)
            sp.dma_start(cst[:], const_sq.rearrange("c p q -> p c q")).then_inc(const_in, 16)
            sp.dma_start(small[:, 0:1], const_col).then_inc(const_in, 16)
            sp.dma_start(gpre_b[:], g_pre.broadcast_to((P, D))).then_inc(const_in, 16)
            sp.dma_start(gsub_b, g_subln.broadcast_to((P, HD))).then_inc(const_in, 16)
            sp.dma_start(lam_in, df_lambda.broadcast_to((P, 4 * DQ))).then_inc(const_in, 16)

            def load_x(t, u):
                sp.dma_start(xb[:, u, :], x[bass.ts(t, P), :]).then_inc(x_in[u], 16)

            load_x(0, 0)
            load_x(1, 1)
            sp.dma_start(w_raw[:], w_wide[0]).then_inc(w_raw_in, 16)
            with sp.Fori(0, SB // 2 - 1) as i:
                for u in range(2):
                    sp.wait_ge(h_rows, i * 2 + (u + 1))
                    load_x(i * 2 + (u + 2), u)

            sp.wait_ge(h_rows, SB)
            sp.wait_ge(ht_ps, 1 + SB)
            sp.wait_ge(const_ok, 8)
            sp.dma_start(red[:].bitcast(I32), positions.broadcast_to((P, S))).then_inc(pos_in, 16)
            with sp.Fori(0, N_V) as c:
                sp.wait_ge(w_lo_ok, c * DC + DC)
                sp.dma_start(w_raw[:], w_wide[c + 1]).then_inc(w_raw_in, 16)
                for b in range(8):
                    sp.wait_ge(vg_ok, c * 8 + (8 + b + 1))
                    for r in range(2):
                        sp.dma_start(v_rows[bass.ds(c * 4, 4), :, 2 * b + r, :].rearrange("h p d -> p h d"),
                                     ring[:, b % 2, r * WIDE:(r + 1) * WIDE].rearrange("p (h d) -> p h d", h=4)
                                     ).then_inc(vg_out[b % 2], 16)

            def store_gates(c):
                for b in range(8):
                    sp.wait_ge(vg_ok, c * 8 + (N_V * 8 + 8 + b + 1))
                    for r in range(2):
                        s = (2 * b + r) * P
                        sp.dma_start(gate_scr[s:s + P, bass.ts(c, WIDE)],
                                     ring[:, b % 2, r * WIDE:(r + 1) * WIDE]).then_inc(vg_out[b % 2], 16)

            with sp.Fori(0, N_G - 1) as c:
                sp.wait_ge(w_lo_ok, c * DC + (N_V + 1) * DC)
                sp.dma_start(w_raw[:], w_wide[c + (N_V + 1)]).then_inc(w_raw_in, 16)
                store_gates(c)
            sp.wait_ge(w_lo_ok, C_SB * DC)
            sp.dma_start(w_raw_n, w_narrow[0]).then_inc(w_raw_in, 16)
            sp.wait_ge(trig_val, 2)
            sp.dma_start(rot_scr[0], turns[:]).then_inc(trig_out, 16)
            sp.dma_start(rot_scr[1], trig[:]).then_inc(trig_out, 16)
            store_gates(N_G - 1)
            for q in range(2):
                sp.wait_ge(vg_out[q], 1 + 32 * 4 * (N_V + N_G))
            sp.wait_ge(trig_out, 32)

            with sp.Fori(0, SB_H) as h:
                sp.wait_ge(sb_o, 1 + h * N_ST)
                sp.dma_start(v1[:, :, 0:HD], v_rows[h]).then_inc(sb_v, 16)
                sp.wait_ge(w_lo_ok, h * DC + (C_SB + 1) * DC)
                sp.dma_start(w_raw_n, w_narrow[h + 1]).then_inc(w_raw_in, 16)
                for t in range(NT):
                    sp.wait_ge(sb_acc, 1 + h * N_ST + (SB_LAST[t] + 1))
                    sp.dma_start(y_rows[t][:, :, bass.ts(h, HD)], acc[:, t % 2]).then_inc(sb_yout[t % 2], 16)

            sp.wait_ge(sb_acc, 1 + SB_H * N_ST)
            sp.dma_start(mem_g, g_mem.broadcast_to((P, D))).then_inc(mm_in, 16)
            sp.dma_start(mem_x, mem[0:P, :]).then_inc(mm_in, 16)
            sp.wait_ge(mm_h, 1)
            sp.dma_start(mem_x, mem[P:2 * P, :]).then_inc(mm_in, 16)
            for c in range(C_MK, C_M):
                sp.wait_ge(w_lo_ok, (c + 1) * DC)
                sp.dma_start(w_raw_n, w_narrow[c + 1 - C_SB]).then_inc(w_raw_in, 16)
            for p in range(2):
                sp.wait_ge(w_lo_ok, (C_M + p + 1) * DC)
                sp.dma_start(w_raw_n, w_narrow[C_M + p + 1 - C_SB]).then_inc(w_raw_in, 16)
                for qb in range(SB):
                    sp.wait_ge(m_y, p * SB + qb + 1)
                    c0 = (SB_H + DF_H + 2 * p) * HD
                    sp.dma_start(y_scr[qb * P:(qb + 1) * P, c0:c0 + 2 * HD].rearrange("p (a d) -> p a d", a=2),
                                 acc[:, qb % 2, 0:2, :]).then_inc(m_yout[qb % 2], 16)

            def differential(h, final):
                for n in range(NT):
                    sp.wait_ge(df_t1, 1 + h * NT + n)
                    sp.wait_ge(df_t2, 1 + h * NT + n)
                    sp.dma_start(w_raw[:, DC * NARROW:].rearrange("p (q s) -> p q s", q=2)[:, 0, :],
                                 rot_scr[0, :, n * TQ:(n + 1) * TQ]).then_inc(df_cs, 16)
                    sp.dma_start(w_raw[:, DC * NARROW:].rearrange("p (q s) -> p q s", q=2)[:, 1, :],
                                 rot_scr[1, :, n * TQ:(n + 1) * TQ]).then_inc(df_cs, 16)
                    if n == 0:
                        sp.wait_ge(df_o, 1 + h * N_DF)
                        sp.dma_start(v1[:, :, 0:HD], v_rows[h + SB_H]).then_inc(df_v, 16)
                if not final:
                    sp.wait_ge(w_lo_ok, h * DC + (C_DF + 1) * DC)
                    sp.dma_start(w_raw_n, w_narrow[h + (C_DF + 1 - C_SB)]).then_inc(w_raw_in, 16)
                for t in range(NT):
                    sp.wait_ge(df_yok, h * NT + (t + 1))
                    sp.dma_start(y_rows[t][:, :, bass.ds(h * HD + SB_H * HD, HD)], acc[:, t % 2]).then_inc(df_yout[t % 2], 16)

            with sp.Fori(0, DF_H - 1) as h:
                differential(h, False)
            differential(DF_H - 1, True)

            for q in range(2):
                sp.wait_ge(sb_yout[q], 1 + 16 * SB_H * NT // 2)
                sp.wait_ge(m_yout[q], 16 * SB)
                sp.wait_ge(df_yout[q], 1 + 16 * DF_H * NT // 2)

            def load_y(t, u):
                sp.dma_start(yb[:, u, :], y_scr[bass.ts(t, P), :]).then_inc(o_in[u], 16)
                sp.dma_start(gb[:, u, :], gate_scr[bass.ts(t, P), :]).then_inc(o_in[u], 16)

            def load_xr(t, u):
                sp.dma_start(xr[:, u, :], x[bass.ts(t, P), :]).then_inc(o_xr[u], 16)

            def store(t, u):
                sp.wait_ge(o_fin, t + 1)
                sp.dma_start(out[bass.ts(t, P), :], ob[:, u, :]).then_inc(o_out[u], 16)

            for u in range(2):
                load_y(u, u)
                load_xr(u, u)
            sp.dma_start(gpost_b[:], g_post.broadcast_to((P, D))).then_inc(gpost_in, 16)
            with sp.Fori(0, SB // 2 - 1) as i:
                for u in range(2):
                    sp.wait_ge(o_tps, i * 2 + (u + 1))
                    load_y(i * 2 + (u + 2), u)
                    store(i * 2 + u, u)
                    load_xr(i * 2 + (u + 2), u)
            for u in range(2):
                store(SB - 2 + u, u)
            for u in range(2):
                sp.wait_ge(o_out[u], 16 * SB // 2)

        @block.tensor
        def _(pe):
            pe.wait_ge(const_ok, 8)

            def transposes(t, u, free):
                pe.wait_ge(h_rows, t + 1)
                for dc in range(DC):
                    if dc % 4 == 0 and free is not None:
                        pe.wait_ge(ht_lo_ok, free + (dc // 4 + 1))
                    mm = pe.transpose(ps[:, 2 * u + dc // 4, (dc % 4) * P:(dc % 4 + 1) * P],
                                      hb[:, u, dc * P:(dc + 1) * P], ident[:])
                mm.then_inc(ht_ps, 1)

            transposes(0, 0, None)
            transposes(1, 1, None)
            with pe.Fori(0, SB // 2 - 1) as i:
                for u in range(2):
                    transposes(i * 2 + (u + 2), u, i * 4 + 2 * u)

            pe.wait_ge(ht_lo_ok, 2 * SB)
            with pe.Fori(0, N_V + N_G) as c:
                for b in range(8):
                    pe.wait_ge(vg_ok, c * 8 + (b + 1))
                    for r in range(2):
                        s = (2 * b + r) * P
                        dst = ps[:, b, r * WIDE:(r + 1) * WIDE]
                        for dc in range(DC):
                            if b == 0 and r == 0:
                                pe.wait_ge(w_lo_ok, c * DC + (dc + 1))
                            pe.matmul(dst, ht_hi[:, dc, s:s + P], w_hi(WIDE, dc), start=(dc == 0), stop=False)
                            pe.matmul(dst, ht_hi[:, dc, s:s + P], w_lo(WIDE, dc), start=False, stop=False)
                            mm = pe.matmul(dst, ht_lo[:, dc, s:s + P], w_hi(WIDE, dc), start=False, stop=(dc == DC - 1))
                            if b == 7 and r == 1 and dc < DC - 1:
                                mm.then_inc(w_free, 1)
                    mm.then_inc(vg_ps, 1)

            def project(c, n, bank, done):
                for dc in range(DC):
                    if n == 0:
                        pe.wait_ge(w_lo_ok, c * DC + (dc + 1))
                    cols = slice(n * TQ, (n + 1) * TQ)
                    pe.matmul(ps[:, bank, :], w_hi(NARROW, dc), ht_hi[:, dc, cols], start=(dc == 0), stop=False)
                    pe.matmul(ps[:, bank, :], w_hi(NARROW, dc), ht_lo[:, dc, cols], start=False, stop=False)
                    mm = pe.matmul(ps[:, bank, :], w_lo(NARROW, dc), ht_hi[:, dc, cols], start=False, stop=(dc == DC - 1))
                    if n == NT - 1 and dc < DC - 1:
                        mm.then_inc(w_free, 1)
                mm.then_inc(done, 1)

            def sb_scores(h, i):
                t, kb, j0 = SB_STEPS[i]
                if kb == 0:
                    pe.wait_ge(sp_act, h * 12 + 3 * (t + 1))
                    pe.wait_ge(sp_dve, h * 8 + 2 * (t + 1))
                if i >= 4:
                    pe.wait_ge(sb_w, h * N_ST + (i - 3))
                z = ps[:, i % 4, j0 * P:TQ]
                cols = slice(t * TQ + j0 * P, (t + 1) * TQ)
                diag = kb >= 4 * t
                pe.matmul(z, sb_s[:, kb * P:(kb + 1) * P], sb_ma[:, cols], start=True, stop=False)
                mm = pe.matmul(z, sb_s[HD:P, kb * P:(kb + 1) * P], sb_mb[HD:P, cols], start=False, stop=True)
                if diag:
                    mm = pe.matmul(ps[:, i % 4, j0 * P:(j0 + 1) * P], ident_b[:], sb_mask[:], start=False, stop=True,
                                   skip_group_check=True)
                mm.then_inc(sb_z, 1)

            def sb_sums(h, i):
                j0 = SB_STEPS[i][2]
                pe.wait_ge(sb_sp, h * N_ST + (i + 1))
                pe.matmul(ps[:, i % 4, j0 * P:TQ], negtri[:], ring[:, i % 3, j0 * P:TQ], start=False, stop=True,
                          skip_group_check=True).then_inc(sb_cum, 1)

            def sb_values(h, i):
                t, kb, j0 = SB_STEPS[i]
                if i == 0:
                    pe.wait_ge(sb_v, h * 16 + 16)
                pe.wait_ge(sb_acc, 1 + h * N_ST + max(0, i - 1))
                pe.wait_ge(sb_w, h * N_ST + (i + 1))
                for j in range(j0, 4):
                    mm = pe.matmul(ps[:, 4 + i % 2, j * (HD + 1):(j + 1) * (HD + 1)], ring[:, 3 + i % 2, j * P:(j + 1) * P],
                                   v1[:, kb, :], start=True, stop=True)
                mm.then_inc(sb_o, 1)

            pe.wait_ge(vg_ok, 8 * (N_V + N_G + 1))
            with pe.Fori(0, SB_H) as h:
                for n in range(NT):
                    if n >= 2:
                        pe.wait_ge(sp_act, h * 12 + 3 * (n - 1))
                        pe.wait_ge(sp_dve, h * 8 + 2 * (n - 1))
                    project(h + C_SB, n, 6 + n % 2, sp_ps)
                for i in range(N_ST + 3):
                    if i < N_ST:
                        sb_scores(h, i)
                    if 2 <= i < N_ST + 2:
                        sb_sums(h, i - 2)
                    if i >= 3:
                        sb_values(h, i - 3)

            for b in range(2):
                pe.wait_ge(mm_h, b + 1)
                for dc in range(DC):
                    if dc % 4 == 0 and b == 1:
                        pe.wait_ge(mm_lo, dc // 4 + 1)
                    mm = pe.transpose(ps[:, dc // 4, (dc % 4) * P:(dc % 4 + 1) * P], mem_h[:, dc * P:(dc + 1) * P], ident[:])
                mm.then_inc(mm_ps, 1)
            pe.wait_ge(mm_lo, 4)
            for k in range(4):
                if k >= 2:
                    pe.wait_ge(mm_ka, k - 1)
                    pe.wait_ge(mm_kd, 2)
                for dc in range(DC):
                    pe.wait_ge(w_lo_ok, (C_MK + k) * DC + dc + 1)
                    for b in range(2 if k >= 2 else 1):
                        first, end = dc == 0, dc == DC - 1
                        if k < 2:
                            dst, rows = ps[:, 2 + k, 0:NMEM], slice(0, NMEM)
                            pe.matmul(dst, w_hi(NARROW, dc), mt_hi[:, dc, rows], start=first, stop=False)
                            pe.matmul(dst, w_hi(NARROW, dc), mt_lo[:, dc, rows], start=False, stop=False)
                            mm = pe.matmul(dst, w_lo(NARROW, dc), mt_hi[:, dc, rows], start=False, stop=end)
                        else:
                            dst, rows = ps[:, 2 * k + b, 0:P], slice(b * P, (b + 1) * P)
                            pe.matmul(dst, mt_hi[:, dc, rows], w_hi(NARROW, dc), start=first, stop=False)
                            pe.matmul(dst, mt_hi[:, dc, rows], w_lo(NARROW, dc), start=False, stop=False)
                            mm = pe.matmul(dst, mt_lo[:, dc, rows], w_hi(NARROW, dc), start=False, stop=end)
                    if dc < DC - 1:
                        mm.then_inc(w_free, 1)
                mm.then_inc(mm_kv, 1)

            for p in range(2):
                if p == 0:
                    pe.wait_ge(mm_ka, 4)
                for n in range(NT):
                    if n < 2:
                        pe.wait_ge(m_y, p * SB)
                    if n >= 2:
                        pe.wait_ge(m_qlo, p * NT + n - 1)
                    project(C_M + p, n, 6 + n % 2, m_pj)
                for i in range(SB + 2):
                    if i < SB:
                        if i % 4 == 0:
                            pe.wait_ge(m_qlo, p * NT + i // 4 + 1)
                        pe.wait_ge(m_p, max(0, p * SB + i - 1))
                        cols = slice(i * P, (i + 1) * P)
                        for a in range(2):
                            dst, half = ps[:, 2 * (i % 2) + a, 0:NMEM], slice(a * HD, (a + 1) * HD)
                            pe.matmul(dst, qm_hi[half, cols], km_hi[half, p, :], start=True, stop=False)
                            pe.matmul(dst, qm_hi[half, cols], km_lo[half, p, :], start=False, stop=False)
                            mm = pe.matmul(dst, qm_lo[half, cols], km_hi[half, p, :], start=False, stop=True)
                        mm.then_inc(m_s, 1)
                    if 1 <= i <= SB:
                        k = i - 1
                        pe.wait_ge(m_pt, max(0, p * SB + k - 1))
                        pe.wait_ge(m_p, p * SB + k + 1)
                        for ab in range(4):
                            mm = pe.transpose(ps[:, 4 + k % 2, ab * P:(ab + 1) * P], ring[:, k % 2, ab * P:(ab + 1) * P], ident[:])
                        mm.then_inc(m_t, 1)
                    if i >= 2:
                        k = i - 2
                        pe.wait_ge(m_y, max(0, p * SB + k - 1))
                        pe.wait_ge(m_pt, p * SB + k + 1)
                        for a in range(2):
                            for b in range(2):
                                mm = pe.matmul(ps[:, 6 + k % 2, a * HD:(a + 1) * HD], ring[:, 2 + k % 2, (2 * a + b) * P:(2 * a + b + 1) * P],
                                               vm[:, b, (2 * p + a) * HD:(2 * p + a + 1) * HD], start=(b == 0), stop=(b == 1))
                        mm.then_inc(m_o, 1)

            def df_unit(h, u):
                kind, t, j, m, c, w = DF_UNITS[u]
                bank = 2 + u % 2
                pe.wait_ge(df_mx, 1 + h * N_UN + max(0, u - 1))
                if kind == "row":
                    pe.wait_ge(df_nm, h * NT + (t + 1))
                    for j in range(4):
                        mm = pe.matmul(ps[0:97, bank, j * P:(j + 1) * P], nm_win[:, m * 4 + j:m * 4 + j + 97], ident_r[:],
                                       start=True, stop=True)
                    mm.then_inc(df_ups, 1)
                    return
                if (j, m, c) == (0, 0, 0):
                    pe.wait_ge(df_pl_a, h * 16 + 4 * (t + 1))
                    pe.wait_ge(df_pl_d, h * 16 + 4 * (t + 1))
                    pe.wait_ge(df_pl_p, 1 + h * 16 + 4 * (t + 1))
                qb = 4 * t + j
                mm = pe.matmul(ps[:, bank, 0:w], df_m[m][:, qb * P:(qb + 1) * P], df_s[m][:, c * TQ:c * TQ + w],
                               start=True, stop=True)
                if c == t:
                    mm = pe.matmul(ps[:, bank, j * P:(j + 1) * P], ident_b[:], df_mask_qk[:], start=False, stop=True,
                                   skip_group_check=True)
                mm.then_inc(df_ups, 1)

            def df_scores(h, i):
                t, kb, j0, m = DF_STEPS[i]
                if kb == 0 and m == 0:
                    pe.wait_ge(df_mx, 1 + h * N_UN + df_unit_range(t)[1])
                if i >= 2:
                    pe.wait_ge(df_e, h * N_DF + (i - 1))
                diag = kb >= 4 * t
                mm = pe.matmul(ps[:, i % 2, j0 * P:TQ], df_s[m][:, kb * P:(kb + 1) * P],
                               df_m[m][:, t * TQ + j0 * P:(t + 1) * TQ], start=True, stop=True)
                if diag:
                    mm = pe.matmul(ps[:, i % 2, j0 * P:(j0 + 1) * P], ident_b[:], df_mask_kq[:], start=False, stop=True,
                                   skip_group_check=True)
                mm.then_inc(df_z, 1)

            def df_values(h, i):
                t, kb, j0, m = DF_STEPS[i]
                if i == 0:
                    pe.wait_ge(df_v, h * 16 + 16)
                if kb == 0 and m == 0:
                    pe.wait_ge(df_fin, 1 + h * NT + max(0, t - 1))
                pe.wait_ge(df_e, h * N_DF + (i + 1))
                for j in range(j0, 4):
                    mm = pe.matmul(ps[:, 4 + 2 * (t % 2) + m, j * (HD + 1):(j + 1) * (HD + 1)], ring[:, i % 3, j * P:(j + 1) * P],
                                   v1[:, kb, :], start=(kb == 0 and j == 0), stop=(kb == 4 * t + j), skip_group_check=True)
                mm.then_inc(df_o, 1)

            def differential(h, final):
                for n in range(NT + 1):
                    if n < NT:
                        if n < 2:
                            pe.wait_ge(df_mx, 1 + h * N_UN)
                        else:
                            pe.wait_ge(df_x, h * NT + (n - 1))
                        project(h + C_DF, n, 2 + n % 2, df_pj)
                    if n >= 1:
                        k = n - 1
                        if k >= 2:
                            pe.wait_ge(df_t2, 1 + h * NT + (k - 1))
                        pe.wait_ge(df_x, h * NT + (k + 1))
                        pe.matmul(ps[:, k % 2, :], rotperm[:], ring[:, k % 2, :], start=True, stop=True).then_inc(df_px, 1)
                pe.wait_ge(df_rows0, h * 2 + 2)
                for what, k in DF_ORDER[final]:
                    if what == "u":
                        df_unit(h, k)
                    if what == "s":
                        df_scores(h, k)
                    if what == "p":
                        df_values(h, k)

            pe.wait_ge(m_y, 2 * SB)
            pe.wait_ge(df_set, 4)
            with pe.Fori(0, DF_H - 1) as h:
                differential(h, False)
            differential(DF_H - 1, True)

            def out_transposes(t, u, free):
                pe.wait_ge(o_yg, t + 1)
                for dc in range(DC):
                    if dc % 4 == 0 and free is not None:
                        pe.wait_ge(o_tlo, free + (dc // 4 + 1))
                    mm = pe.transpose(ps[:, 2 * u + dc // 4, (dc % 4) * P:(dc % 4 + 1) * P],
                                      yb[:, u, dc * P:(dc + 1) * P], ident[:])
                mm.then_inc(o_tps, 1)

            def out_products(t, u, free):
                pe.wait_ge(o_tlo, t * 2 + 2)
                for g in range(2):
                    if free is not None:
                        pe.wait_ge(o_n, free + (g + 1))
                    dst, cols = ps[:, 4 + 2 * u + g, :], slice(g * 512, (g + 1) * 512)
                    for dc in range(DC):
                        pe.matmul(dst, yt_hi[:, u, dc, :], wo_hi[:, dc, cols], start=(dc == 0), stop=False)
                        pe.matmul(dst, yt_hi[:, u, dc, :], wo_lo[:, dc, cols], start=False, stop=False)
                        mm = pe.matmul(dst, yt_lo[:, u, dc, :], wo_hi[:, dc, cols], start=False, stop=(dc == DC - 1))
                    mm.then_inc(o_ps, 1)

            pe.wait_ge(df_fin, 1 + DF_H * NT)
            out_transposes(0, 0, None)
            out_transposes(1, 1, None)
            pe.wait_ge(wo_lo_ok, DC)
            out_products(0, 0, None)
            out_transposes(2, 0, 0)
            out_products(1, 1, None)
            with pe.Fori(0, SB // 2 - 2) as i:
                for u in range(2):
                    out_transposes(i * 2 + (u + 3), 1 - u, i * 4 + (2 * u + 2))
                    out_products(i * 2 + (u + 2), u, i * 4 + 2 * u)
            out_transposes(SB - 1, 1, 2 * (SB - 3))
            out_products(SB - 2, 0, 2 * (SB - 4))
            out_products(SB - 1, 1, 2 * (SB - 3))

        @block.scalar
        def _(act):
            act.preload_act_table_set("natural_log_exp_and_others")

            def split_hi(c, cols, dc, free, whole=False):
                if dc == 0:
                    act.wait_ge(w_raw_in, c * 16 + 16)
                if free is not None:
                    done, value = free
                    if dc < DC - 1 and not whole:
                        act.wait_ge(w_free, c * (DC - 1) + (dc + 1 - (DC - 1)))
                    else:
                        act.wait_ge(done, value)
                nc.scalar.activation(w_hi(cols, dc), raw(cols, dc), ACT.Copy).then_inc(w_hi_ok, 1)

            def rsqrt_of(var, ln, y0, var_ok, n, ln_ok, y0_ok):
                act.wait_ge(var_ok, n)
                nc.scalar.activation(ln, var, ACT.Ln).then_inc(ln_ok, 1)
                act.wait_ge(ln_ok, n)
                nc.scalar.activation(y0, ln, ACT.Exp, scale=-0.5).then_inc(y0_ok, 1)

            def norm_square(t, u):
                act.wait_ge(x_in[u], (t - u) * 8 + 16)
                act.wait_ge(ht_ps, 1 + t - 1) if not isinstance(t, int) or t >= 2 else None
                nc.scalar.activation(hb[:, u, :], xb[:, u, :], ACT.Square, accum_out=col(0, u)).then_inc(x_sq, 1)

            def norm_hi(t, u):
                act.wait_ge(ht_ps, 1 + t + 1)
                for g in range(2):
                    nc.scalar.activation(ht_hi[:, 4 * g:4 * g + 4, bass.ts(t, P)],
                                         ps[:, 2 * u + g, :].rearrange("p (c s) -> p c s", c=4), ACT.Copy).then_inc(ht_hi_ok, 1)

            act.wait_ge(lam_ch, 2)
            nc.scalar.activation(small[:, 2:4], small[:, 4:6], ACT.Exp).then_inc(lam_e, 1)
            norm_square(0, 0)
            rsqrt_of(col(1, 0), col(2, 0), col(3, 0), x_var, 1, x_ln, x_y0)
            for dc in range(DC):
                split_hi(0, WIDE, dc, None)
            with act.Fori(0, SB // 2 - 1) as i:
                for q in range(2):
                    u = 1 - q
                    act.wait_ge(x_in[u], i * 16 + 16 * (q + 1))
                    act.wait_ge(ht_ps, 1 + i * 2 + q)
                    nc.scalar.activation(hb[:, u, :], xb[:, u, :], ACT.Square, accum_out=col(0, u)).then_inc(x_sq, 1)
                    norm_hi(i * 2 + q, 1 - u)
                    rsqrt_of(col(1, u), col(2, u), col(3, u), x_var, i * 2 + (q + 2), x_ln, x_y0)
            act.wait_ge(x_in[1], 16 * SB // 2)
            act.wait_ge(ht_ps, 1 + SB - 2)
            nc.scalar.activation(hb[:, 1, :], xb[:, 1, :], ACT.Square, accum_out=col(0, 1)).then_inc(x_sq, 1)
            norm_hi(SB - 2, 0)
            rsqrt_of(col(1, 1), col(2, 1), col(3, 1), x_var, SB, x_ln, x_y0)
            norm_hi(SB - 1, 1)

            act.sem_inc(vg_ok, 8)
            act.wait_ge(trig_ch, 10)
            nc.scalar.activation(trig[:], red[:], ACT.Sin).then_inc(trig_val, 1)
            nc.scalar.activation(turns[:], ang[:], ACT.Sin).then_inc(trig_val, 1)
            act.preload_act_table_set("natural_log_exp_and_others")

            def vg_last(c):
                return (vg_ps, c * 8)

            with act.Fori(0, N_V) as c:
                for b in range(8):
                    if b == 7:
                        for dc in range(DC):
                            split_hi(c + 1, WIDE, dc, (vg_ps, c * 8 + 8))
                    act.wait_ge(vg_out[b % 2], 1 + c * 128 + 32 * (b // 2))
                    act.wait_ge(vg_ps, c * 8 + (b + 1))
                    nc.scalar.activation(ring[:, b % 2, :], ps[:, b, :], ACT.Copy).then_inc(vg_ok, 1)

            def gates(c, cols):
                for b in range(8):
                    if b == 7:
                        for dc in range(DC):
                            split_hi(c + (N_V + 1), cols, dc, (vg_ps, c * 8 + (N_V * 8 + 8)), whole=cols == NARROW)
                    act.wait_ge(vg_ok, c * 8 + (N_V * 8 + 8 + b - 1))
                    act.wait_ge(vg_ps, c * 8 + (N_V * 8 + b + 1))
                    nc.scalar.activation(ring[:, 2 + b % 2, :], ps[:, b, :], ACT.Exp, scale=-1.0).then_inc(vg_e, 1)

            with act.Fori(0, N_G - 1) as c:
                gates(c, WIDE)
            gates(N_G - 1, NARROW)

            def sb_exp_z(h, i):
                j0 = SB_STEPS[i][2]
                if i >= 3:
                    act.wait_ge(sb_cum, h * N_ST + (i - 2))
                act.wait_ge(sb_z, h * N_ST + (i + 1))
                nc.scalar.activation(ring[:, i % 3, j0 * P:], ps[:, i % 4, j0 * P:], ACT.Exp).then_inc(sb_e, 1)

            def sb_log(h, i):
                j0 = SB_STEPS[i][2]
                act.wait_ge(sb_clamp, h * N_ST + (i + 1))
                nc.scalar.activation(ring[:, i % 3, j0 * P:], ring[:, i % 3, j0 * P:], ACT.Ln, bias=1.0).then_inc(sb_ln, 1)

            def sb_exp_w(h, i):
                j0 = SB_STEPS[i][2]
                if i >= 2:
                    act.wait_ge(sb_o, 1 + h * N_ST + (i - 1))
                act.wait_ge(sb_cum, h * N_ST + (i + 1))
                nc.scalar.activation(ring[:, 3 + i % 2, j0 * P:], ps[:, i % 4, j0 * P:], ACT.Exp).then_inc(sb_w, 1)

            act.wait_ge(trig_out, 32)
            for q in range(2):
                act.wait_ge(vg_out[q], 1 + 32 * 4 * (N_V + N_G))
            with act.Fori(0, SB_H) as h:
                for n in range(NT):
                    cols = slice(n * TQ, (n + 1) * TQ)
                    act.wait_ge(sp_ps, h * NT + (n + 1))
                    nc.scalar.activation(sb_ma[0:HD, cols], ps[0:HD, 6 + n % 2, :], ACT.Copy, scale=HD ** -0.5).then_inc(sp_act, 1)
                    nc.scalar.activation(sb_s[HD:P, cols], ps[HD:P, 6 + n % 2, :], ACT.Copy).then_inc(sp_act, 1)
                    nc.scalar.activation(sb_ma[HD:P, cols], ps[0:HD, 6 + n % 2, :], ACT.Copy, scale=HD ** -0.5).then_inc(sp_act, 1)
                for i in range(N_ST + 2):
                    if i < N_ST:
                        sb_exp_z(h, i)
                    if 1 <= i <= N_ST:
                        sb_log(h, i - 1)
                    if i >= 2:
                        sb_exp_w(h, i - 2)
                    if 4 <= i < 4 + DC:
                        split_hi(h + (C_SB + 1), NARROW, i - 4, (sp_ps, h * NT + NT))

            for b in range(2):
                act.wait_ge(mm_in, 32 + 16 * b)
                if b:
                    act.wait_ge(mm_ps, 1)
                nc.scalar.activation(mem_h, mem_x, ACT.Square, accum_out=col(0, b)).then_inc(mm_sq, 1)
                rsqrt_of(col(1, b), col(2, b), col(3, b), mm_ch, 5 * b + 1, mm_ln, mm_y0) if b == 0 else None
                if b:
                    act.wait_ge(mm_ch, 6)
                    nc.scalar.activation(col(2, 1), col(1, 1), ACT.Ln).then_inc(mm_ln, 1)
                    act.wait_ge(mm_ln, 2)
                    nc.scalar.activation(col(3, 1), col(2, 1), ACT.Exp, scale=-0.5).then_inc(mm_y0, 1)
                act.wait_ge(mm_ps, b + 1)
                for g in range(2):
                    nc.scalar.activation(mt_hi[:, 4 * g:4 * g + 4, b * P:(b + 1) * P],
                                         ps[:, g, :].rearrange("p (c s) -> p c s", c=4), ACT.Copy).then_inc(mm_hi, 1)
            for k in range(4):
                for dc in range(DC):
                    split_hi(C_MK + k + 1, NARROW, dc, (mm_kv, k + 1))
                act.wait_ge(mm_kv, k + 1)
                if k < 2:
                    nc.scalar.activation(km_hi[:, k, :], ps[:, 2 + k, 0:NMEM], ACT.Copy).then_inc(mm_ka, 1)
                else:
                    nc.scalar.activation(vm[:, :, (k - 2) * P:(k - 1) * P], ps[:, 2 * k:2 * k + 2, 0:P], ACT.Copy).then_inc(mm_ka, 1)

            for p in range(2):
                for n in range(NT):
                    act.wait_ge(m_pj, p * NT + n + 1)
                    nc.scalar.activation(qm_hi[:, n * TQ:(n + 1) * TQ], ps[:, 6 + n % 2, :], ACT.Copy, scale=HD ** -0.5).then_inc(m_qhi, 1)
                for i in range(SB + 1):
                    if i < SB:
                        act.wait_ge(m_nm, p * SB + i + 1)
                        act.wait_ge(m_t, max(0, p * SB + i - 1))
                        act.wait_ge(m_y, max(0, p * SB + i - 1))
                        for a in range(2):
                            e = nc.scalar.activation(ring[:, i % 2, a * NMEM:(a + 1) * NMEM], ps[:, 2 * (i % 2) + a, 0:NMEM],
                                                     ACT.Exp, bias=col(1, i % 2, 2)[:, a:a + 1], accum_out=col(2, i % 2, 2)[:, a:a + 1])
                        e.then_inc(m_p, 1)
                    if i >= 1:
                        k = i - 1
                        act.wait_ge(m_t, p * SB + k + 1)
                        act.wait_ge(m_o, max(0, p * SB + k - 1))
                        nc.scalar.activation(ring[:, 2 + k % 2, :], ps[:, 4 + k % 2, :], ACT.Copy).then_inc(m_pt, 1)
                    if 4 <= i < 4 + DC:
                        split_hi(C_M + p + 1, NARROW, i - 4, (m_pj, (p + 1) * NT))

            def df_place_hi(h, n):
                cols = slice(n * TQ, (n + 1) * TQ)
                if n >= 2:
                    act.wait_ge(df_pl_d, h * 16 + 4 * (n - 1))
                    act.wait_ge(df_lo, h * NT + (n - 1))
                act.wait_ge(df_x2, h * NT + (n + 1))
                nc.scalar.activation(hi_tmp[:, n % 2, :], ring[:, 4 + n % 2, :], ACT.Copy).then_inc(df_hi, 1)
                act.wait_ge(df_hi, h * NT + (n + 1))
                for m in range(2):
                    for r in (0, 2 * DQ):
                        k0 = 2 * DQ + m * DQ
                        nc.scalar.activation(df_s[m][r:r + DQ, cols], hi_tmp[k0:k0 + DQ, n % 2, :].bitcast(F32), ACT.Copy).then_inc(df_pl_a, 1)

            def df_exp(h, i):
                j0 = DF_STEPS[i][2]
                act.wait_ge(df_o, 1 + h * N_DF + max(0, i - 2))
                act.wait_ge(df_z, h * N_DF + (i + 1))
                nc.scalar.activation(ring[:, i % 3, j0 * P:], ps[:, i % 2, j0 * P:], ACT.Exp, scale=DQ ** -0.5).then_inc(df_e, 1)

            def differential(h, final):
                for n in range(NT + 1):
                    if n < NT:
                        if n >= 2:
                            act.wait_ge(df_t1, 1 + h * NT + (n - 1))
                            act.wait_ge(df_px, h * NT + (n - 1))
                        act.wait_ge(df_pj, h * NT + (n + 1))
                        nc.scalar.activation(ring[:, n % 2, :], ps[:, 2 + n % 2, :], ACT.Copy).then_inc(df_x, 1)
                    if n >= 1:
                        df_place_hi(h, n - 1)
                for what, k in DF_ORDER[final]:
                    if what == "s":
                        df_exp(h, k)
                        if not final and 8 <= k < 8 + DC:
                            split_hi(h + (C_DF + 1), NARROW, k - 8, (df_pj, h * NT + NT))
                    if what == "l":
                        rsqrt_of(col(4, 0, 4), col(5, 0, 4), col(6, 0, 4), df_var, h * NT + (k + 1), df_ln, df_y0)
                    if what == "w":
                        act.wait_ge(wo_in[k % 2], 16 * (k // 2 + 1))
                        nc.scalar.activation(wo_hi[:, k, :], w_raw[:, (k % 2) * D:(k % 2 + 1) * D], ACT.Copy).then_inc(wo_hi_ok, 1)

            with act.Fori(0, DF_H - 1) as h:
                differential(h, False)
            differential(DF_H - 1, True)

            def out_hi(t, u, free):
                act.wait_ge(o_tps, t + 1)
                if free is not None:
                    act.wait_ge(o_ps, free)
                for g in range(2):
                    nc.scalar.activation(yt_hi[:, u, 4 * g:4 * g + 4, :],
                                         ps[:, 2 * u + g, :].rearrange("p (c s) -> p c s", c=4), ACT.Copy).then_inc(o_thi, 1)

            def out_square(t, u, free):
                if free is not None:
                    act.wait_ge(o_out[u], free)
                    act.wait_ge(o_fin, t - 1)
                for g in range(2):
                    act.wait_ge(o_ps, t * 2 + (g + 1))
                    nc.scalar.activation(ob[:, u, g * 512:(g + 1) * 512], ps[:, 4 + 2 * u + g, :], ACT.Square,
                                         accum_out=col(g, u)).then_inc(o_sq, 1)
                rsqrt_of(col(2, u), col(3, u), col(4, u), o_var, t + 1, o_ln, o_y0)

            out_hi(0, 0, None)
            out_hi(1, 1, None)
            out_square(0, 0, None)
            out_hi(2, 0, 2)
            out_square(1, 1, None)
            with act.Fori(0, SB // 2 - 2) as i:
                for u in range(2):
                    out_hi(i * 2 + (u + 3), 1 - u, i * 4 + (2 * u + 4))
                    out_square(i * 2 + (u + 2), u, i * 16 + 16)
            out_hi(SB - 1, 1, 2 * (SB - 2))
            out_square(SB - 2, 0, 16 * (SB // 2 - 1))
            out_square(SB - 1, 1, 16 * (SB // 2 - 1))

        @block.vector
        def _(dve):
            def split_lo(c, cols, dc):
                dve.wait_ge(w_hi_ok, c * DC + (dc + 1))
                nc.vector.tensor_tensor(w_lo(cols, dc), raw(cols, dc), w_hi(cols, dc).bitcast(F32), ALU.subtract).then_inc(w_lo_ok, 1)

            def newton(var, y0, tmp, y, chain, n):
                nc.vector.tensor_tensor(tmp, y0, y0, ALU.mult).then_inc(chain, 1)
                dve.wait_ge(chain, n + 1)
                nc.vector.tensor_tensor(tmp, tmp, var, ALU.mult).then_inc(chain, 1)
                dve.wait_ge(chain, n + 2)
                nc.vector.tensor_scalar(tmp, tmp, -0.5, 1.5, ALU.mult, ALU.add).then_inc(chain, 1)
                dve.wait_ge(chain, n + 3)
                nc.vector.tensor_tensor(y, tmp, y0, ALU.mult).then_inc(chain, 1)
                dve.wait_ge(chain, n + 4)

            dve.wait_ge(const_in, 80)
            for k, dst in enumerate((ident, negtri, rotperm, ident_b, sb_mask, df_mask_kq, df_mask_qk, ident_r)):
                src = (0, 1, 2, 0, 3, 4, 5, 0)[k]
                nc.vector.tensor_copy(dst[:], cst[:, src, :]).then_inc(const_ok, 1)
            nc.vector.memset(v1[:, :, HD:HD + 1], 1.0).then_inc(lam_ch, 1)
            lam4 = lam_in.rearrange("p (a b d) -> p a b d", a=2, b=2)
            prod = ring[:, 0, 0:2 * DQ].rearrange("p (a d) -> p a d", a=2)
            nc.vector.tensor_tensor(prod, lam4[:, :, 0, :], lam4[:, :, 1, :], ALU.mult).then_inc(sb_ch, 1)
            dve.wait_ge(sb_ch, 1)
            nc.vector.tensor_reduce(small[:, 4:6], prod, AXX, ALU.add).then_inc(lam_ch, 1)
            nc.vector.tensor_scalar(gsub_b, gsub_b, 1.0 - LAMBDA_INIT, None, ALU.mult).then_inc(sb_ch, 1)

            def norm_var(t, u):
                dve.wait_ge(x_sq, t + 1)
                nc.vector.tensor_scalar(col(1, u), col(0, u), 1.0 / D, EPS, ALU.mult, ALU.add).then_inc(x_var, 1)

            def norm_rows(t, u):
                dve.wait_ge(x_y0, t + 1)
                newton(col(1, u), col(3, u), col(4, u), col(5, u), x_nr, t * 4)
                nc.vector.scalar_tensor_tensor(out=hb[:, u, :], in0=xb[:, u, :], scalar=col(5, u), in1=gpre_b[:],
                                               op0=ALU.mult, op1=ALU.mult).then_inc(h_rows, 1)

            def norm_lo(t, u):
                for g in range(2):
                    dve.wait_ge(ht_hi_ok, t * 2 + (g + 1))
                    rows = (slice(None), slice(4 * g, 4 * g + 4), bass.ts(t, P))
                    nc.vector.tensor_tensor(ht_lo[rows], ps[:, 2 * u + g, :].rearrange("p (c s) -> p c s", c=4),
                                            ht_hi[rows].bitcast(F32), ALU.subtract).then_inc(ht_lo_ok, 1)

            norm_var(0, 0)
            norm_rows(0, 0)
            dve.wait_ge(lam_e, 1)
            nc.vector.tensor_tensor(small[:, 6:7], small[:, 2:3], small[:, 3:4], ALU.subtract).then_inc(sb_ch, 1)
            dve.wait_ge(sb_ch, 3)
            nc.vector.tensor_scalar(lam, small[:, 6:7], LAMBDA_INIT, None, ALU.add).then_inc(sb_ch, 1)
            for dc in range(DC):
                split_lo(0, WIDE, dc)
            with dve.Fori(0, SB // 2 - 1) as i:
                for q in range(2):
                    norm_var(i * 2 + (q + 1), 1 - q)
                    norm_lo(i * 2 + q, q)
                    norm_rows(i * 2 + (q + 1), 1 - q)
            norm_var(SB - 1, 1)
            norm_lo(SB - 2, 0)
            norm_rows(SB - 1, 1)
            norm_lo(SB - 1, 1)

            two_pi = 2 * math.pi
            c1 = 201 / 32
            c2 = round((two_pi - c1) * 2 ** 21) / 2 ** 21
            c3 = two_pi - c1 - c2
            magic = 1.5 * 2 ** 23
            pi_in = 3.1415925
            dve.wait_ge(pos_in, 16)
            nc.vector.tensor_scalar(ang[:], red[:].bitcast(I32), invf, None, ALU.mult).then_inc(trig_ch, 1)
            dve.wait_ge(trig_ch, 1)
            nc.vector.tensor_scalar(turns[:], ang[:], 1 / two_pi, magic, ALU.mult, ALU.add).then_inc(trig_ch, 1)
            dve.wait_ge(trig_ch, 2)
            nc.vector.tensor_scalar(turns[:], turns[:], magic, None, ALU.subtract).then_inc(trig_ch, 1)
            dve.wait_ge(trig_ch, 3)
            for k, (part, base) in enumerate(((c1, ang), (c2, red), (c3, red))):
                nc.vector.scalar_tensor_tensor(out=red[:], in0=turns[:], scalar=-part, in1=base[:],
                                               op0=ALU.mult, op1=ALU.add).then_inc(trig_ch, 1)
                dve.wait_ge(trig_ch, 4 + k)
            nc.vector.tensor_scalar(turns[:], red[:], math.pi / 2, -two_pi, ALU.is_gt, ALU.mult).then_inc(trig_ch, 1)
            dve.wait_ge(trig_ch, 7)
            nc.vector.scalar_tensor_tensor(out=ang[:], in0=red[:], scalar=math.pi / 2, in1=turns[:],
                                           op0=ALU.add, op1=ALU.add).then_inc(trig_ch, 1)
            dve.wait_ge(trig_ch, 8)
            nc.vector.tensor_scalar(red[:], red[:], pi_in, -pi_in, ALU.min, ALU.max).then_inc(trig_ch, 1)
            nc.vector.tensor_scalar(ang[:], ang[:], pi_in, -pi_in, ALU.min, ALU.max).then_inc(trig_ch, 1)

            with dve.Fori(0, N_V) as c:
                for dc in range(DC):
                    split_lo(c + 1, WIDE, dc)

            def gates(c, cols):
                for b in range(8):
                    if b == 7:
                        for dc in range(DC):
                            split_lo(c + (N_V + 1), cols, dc)
                    e = ring[:, 2 + b % 2, :]
                    dve.wait_ge(vg_e, c * 8 + (b + 1))
                    nc.vector.tensor_scalar(e, e, 1.0, None, ALU.add).then_inc(vg_ch, 1)
                    dve.wait_ge(vg_ch, c * 16 + (2 * b + 1))
                    nc.vector.reciprocal(e, e).then_inc(vg_ch, 1)
                    dve.wait_ge(vg_out[b % 2], 1 + c * 128 + (128 * N_V + 32 * (b // 2)))
                    dve.wait_ge(vg_ch, c * 16 + (2 * b + 2))
                    nc.vector.tensor_tensor(ring[:, b % 2, :], ps[:, b, :], e, ALU.mult).then_inc(vg_ok, 1)

            with dve.Fori(0, N_G - 1) as c:
                gates(c, WIDE)
            gates(N_G - 1, NARROW)

            def sb_softplus(h, i):
                j0 = SB_STEPS[i][2]
                dve.wait_ge(sb_ln, h * N_ST + (i + 1))
                sp_ = ring[:, i % 3, j0 * P:]
                nc.vector.tensor_tensor(sp_, ps[:, i % 4, j0 * P:], sp_, ALU.max).then_inc(sb_sp, 1)

            def sb_add(h, i):
                t, kb, j0 = SB_STEPS[i]
                o = ps[:, 4 + i % 2, 0:4 * (HD + 1)].rearrange("p (j d) -> p j d", j=4)[:, j0:, :]
                a = acc[:, t % 2, j0:, :]
                left = small[:, 60:64][:, j0:]
                dve.wait_ge(sb_o, 1 + h * N_ST + (i + 1))
                if kb == 0:
                    dve.wait_ge(sb_yout[t % 2], 1 + h * 32 + (16 if t >= 2 else 0))
                    nc.vector.tensor_copy(a, o[:, :, 0:HD]).then_inc(sb_acc, 1)
                    return
                before = 4 + 2 * SB_MULS.index(i)
                chain = h * (2 * len(SB_MULS))
                nc.vector.tensor_scalar(left, o[:, :, HD], -1.0, 1.0, ALU.mult, ALU.add).then_inc(sb_ch, 1)
                dve.wait_ge(sb_acc, 1 + h * N_ST + i)
                dve.wait_ge(sb_ch, chain + (before + 1))
                nc.vector.tensor_tensor(a, a, left.unsqueeze(2).broadcast_to((P, 4 - j0, HD)), ALU.mult).then_inc(sb_ch, 1)
                dve.wait_ge(sb_ch, chain + (before + 2))
                nc.vector.tensor_tensor(a, o[:, :, 0:HD], a, ALU.add).then_inc(sb_acc, 1)

            with dve.Fori(0, SB_H) as h:
                for n in range(NT):
                    cols = slice(n * TQ, (n + 1) * TQ)
                    dve.wait_ge(sp_act, h * 12 + (3 * n + 3))
                    nc.vector.scalar_tensor_tensor(out=sb_mb[HD:P, cols], in0=ps[0:HD, 6 + n % 2, :], scalar=HD ** -0.5,
                                                   in1=sb_ma[0:HD, cols].bitcast(F32), op0=ALU.mult, op1=ALU.subtract).then_inc(sp_dve, 1)
                    nc.vector.tensor_tensor(sb_s[0:HD, cols], ps[HD:P, 6 + n % 2, :], sb_s[HD:P, cols].bitcast(F32),
                                            ALU.subtract).then_inc(sp_dve, 1)
                for i in range(1, N_ST + 3):
                    if i <= N_ST:
                        sb_softplus(h, i - 1)
                    if i >= 3:
                        sb_add(h, i - 3)
                    if 5 <= i < 5 + DC:
                        split_lo(h + (C_SB + 1), NARROW, i - 5)

            for b in range(2):
                dve.wait_ge(mm_sq, b + 1)
                nc.vector.tensor_scalar(col(1, b), col(0, b), 1.0 / D, EPS, ALU.mult, ALU.add).then_inc(mm_ch, 1)
                dve.wait_ge(mm_y0, b + 1)
                newton(col(1, b), col(3, b), col(4, b), col(5, b), mm_ch, 5 * b + 1)
                nc.vector.scalar_tensor_tensor(out=mem_h, in0=mem_x, scalar=col(5, b), in1=mem_g,
                                               op0=ALU.mult, op1=ALU.mult).then_inc(mm_h, 1)
                for g in range(2):
                    dve.wait_ge(mm_hi, 2 * b + g + 1)
                    rows = (slice(None), slice(4 * g, 4 * g + 4), slice(b * P, (b + 1) * P))
                    nc.vector.tensor_tensor(mt_lo[rows], ps[:, g, :].rearrange("p (c s) -> p c s", c=4),
                                            mt_hi[rows].bitcast(F32), ALU.subtract).then_inc(mm_lo, 1)
            for k in range(4):
                for dc in range(DC):
                    split_lo(C_MK + k + 1, NARROW, dc)
                if k < 2:
                    dve.wait_ge(mm_ka, k + 1)
                    nc.vector.tensor_tensor(km_lo[:, k, :], ps[:, 2 + k, 0:NMEM], km_hi[:, k, :].bitcast(F32), ALU.subtract).then_inc(mm_kd, 1)

            for p in range(2):
                for n in range(NT):
                    cols = slice(n * TQ, (n + 1) * TQ)
                    dve.wait_ge(m_qhi, p * NT + n + 1)
                    nc.vector.scalar_tensor_tensor(out=qm_lo[:, cols], in0=ps[:, 6 + n % 2, :], scalar=HD ** -0.5,
                                                   in1=qm_hi[:, cols].bitcast(F32), op0=ALU.mult, op1=ALU.subtract).then_inc(m_qlo, 1)
                for i in range(SB + 2):
                    if i < SB:
                        dve.wait_ge(m_s, p * SB + i + 1)
                        nc.vector.tensor_reduce(col(0, i % 2, 2), ps[:, 2 * (i % 2):2 * (i % 2) + 2, 0:NMEM], AXX, ALU.max).then_inc(m_mx, 1)
                        dve.wait_ge(m_mx, p * SB + i + 1)
                        dve.wait_ge(m_p, max(0, p * SB + i - 1))
                        nc.vector.tensor_scalar(col(1, i % 2, 2), col(0, i % 2, 2), -1.0, None, ALU.mult).then_inc(m_nm, 1)
                    if i >= 2:
                        k = i - 2
                        dve.wait_ge(m_o, p * SB + k + 1)
                        dve.wait_ge(m_yout[k % 2], 16 * (p * SB // 2 + k // 2))
                        nc.vector.reciprocal(col(3, k % 2, 2), col(2, k % 2, 2)).then_inc(m_rc, 1)
                        dve.wait_ge(m_rc, p * SB + k + 1)
                        nc.vector.tensor_tensor(acc[:, k % 2, 0:2, :], ps[:, 6 + k % 2, 0:2 * HD].rearrange("p (a d) -> p a d", a=2),
                                                col(3, k % 2, 2).unsqueeze(2).broadcast_to((P, 2, HD)), ALU.mult).then_inc(m_y, 1)
                    if 5 <= i < 5 + DC:
                        split_lo(C_M + p + 1, NARROW, i - 5)

            pmax = ring[:, 5, 0:32].rearrange("p (m j c) -> p m j c", m=2, j=4)
            mx8 = ring[:, 5, 32:40]
            rc = ring[:, 5, 40:48].rearrange("p (m j) -> p m j", m=2)
            second = ring[:, 3, 0:256].rearrange("p (j d) -> p j d", j=4)
            square = ring[:, 3, 256:512].rearrange("p (j d) -> p j d", j=4)

            def df_rotate(h, n):
                cols = slice(n * TQ, (n + 1) * TQ)
                x2 = ring[:, 4 + n % 2, :]
                dve.wait_ge(df_px, h * NT + (n + 1))
                if n >= 2:
                    dve.wait_ge(df_hi, h * NT + (n - 1))
                nc.vector.tensor_tensor(x2, ps[:, n % 2, :], sin_c, ALU.mult).then_inc(df_t2, 1)
                dve.wait_ge(df_t2, 1 + h * NT + (n + 1))
                dve.wait_ge(df_t1, 1 + h * NT + (n + 1))
                nc.vector.tensor_tensor(x2, x2, ring[:, 2 + n % 2, :], ALU.add).then_inc(df_x2, 1)
                dve.wait_ge(df_hi, h * NT + (n + 1))
                if n >= 2:
                    dve.wait_ge(df_pl_p, 1 + h * 16 + 4 * (n - 1))
                nc.vector.tensor_tensor(lo_tmp[:, n % 2, :], x2, hi_tmp[:, n % 2, :].bitcast(F32), ALU.subtract).then_inc(df_lo, 1)
                for m in range(2):
                    for r in (0, DQ):
                        nc.vector.tensor_copy(df_m[m][r:r + DQ, cols], hi_tmp[m * DQ:(m + 1) * DQ, n % 2, :].bitcast(F32)).then_inc(df_pl_d, 1)

            def df_unit(h, u):
                kind, t, j, m, c, w = DF_UNITS[u]
                dve.wait_ge(df_ups, h * N_UN + (u + 1))
                if kind == "row":
                    nc.vector.tensor_copy(df_m[m][96:97, t * TQ:(t + 1) * TQ], ps[96:97, 2 + u % 2, :]).then_inc(df_mx, 1)
                    return
                nc.vector.tensor_reduce(pmax[:, m, j, c:c + 1], ps[:, 2 + u % 2, 0:w], AXX, ALU.max).then_inc(df_mx, 1)
                if DF_UNITS[u + 1][0] == "row":
                    dve.wait_ge(df_mx, 1 + h * N_UN + (u + 1))
                    nc.vector.tensor_reduce(mx8, pmax.rearrange("p m j c -> p (m j) c")[:, :, 0:t + 1], AXX, ALU.max).then_inc(df_cb, 1)
                    dve.wait_ge(df_cb, h * NT + (t + 1))
                    nc.vector.tensor_scalar(nm_win[:, 96:104], mx8, -1.0, None, ALU.mult).then_inc(df_nm, 1)

            def df_end(h, t):
                o = [ps[:, 4 + 2 * (t % 2) + m, 0:4 * (HD + 1)].rearrange("p (j d) -> p j d", j=4) for m in range(2)]
                a, ch = acc[:, t % 2], h * 24 + 6 * t
                dve.wait_ge(df_o, 1 + h * N_DF + (max(i for i, s in enumerate(DF_STEPS) if s[0] == t) + 1))
                dve.wait_ge(df_yout[t % 2], 1 + h * 32 + (16 if t >= 2 else 0))
                for m in range(2):
                    nc.vector.reciprocal(rc[:, m, :], o[m][:, :, HD]).then_inc(df_fch, 1)
                dve.wait_ge(df_fch, ch + 2)
                nc.vector.tensor_scalar(rc[:, 1, :], rc[:, 1, :], lam, None, ALU.mult).then_inc(df_fch, 1)
                nc.vector.tensor_tensor(a, o[0][:, :, 0:HD], rc[:, 0, :].unsqueeze(2).broadcast_to((P, 4, HD)), ALU.mult).then_inc(df_fch, 1)
                dve.wait_ge(df_fch, ch + 4)
                nc.vector.tensor_tensor(second, o[1][:, :, 0:HD], rc[:, 1, :].unsqueeze(2).broadcast_to((P, 4, HD)), ALU.mult).then_inc(df_fin, 1)
                dve.wait_ge(df_fin, 1 + h * NT + (t + 1))
                nc.vector.tensor_tensor(a, a, second, ALU.subtract).then_inc(df_fch, 1)
                dve.wait_ge(df_fch, ch + 5)
                nc.vector.tensor_tensor(square, a, a, ALU.mult).then_inc(df_fch, 1)
                dve.wait_ge(df_fch, ch + 6)
                nc.vector.tensor_reduce(col(3, 0, 4), square, AXX, ALU.add).then_inc(df_gch, 1)
                dve.wait_ge(df_gch, h * 24 + (6 * t + 1))
                nc.vector.tensor_scalar(col(4, 0, 4), col(3, 0, 4), 1.0 / HD, EPS, ALU.mult, ALU.add).then_inc(df_var, 1)

            def df_norm(h, t):
                a = acc[:, t % 2]
                dve.wait_ge(df_y0, h * NT + (t + 1))
                newton(col(4, 0, 4), col(6, 0, 4), col(5, 1, 4), col(6, 1, 4), df_gch, h * 24 + (6 * t + 1))
                nc.vector.tensor_tensor(a, a, col(6, 1, 4).unsqueeze(2).broadcast_to((P, 4, HD)), ALU.mult).then_inc(df_gch, 1)
                dve.wait_ge(df_gch, h * 24 + (6 * t + 6))
                nc.vector.tensor_tensor(a, a, gsub_b.unsqueeze(1).broadcast_to((P, 4, HD)), ALU.mult).then_inc(df_yok, 1)

            def differential(h, final):
                for n in range(NT + 1):
                    if n < NT:
                        dve.wait_ge(df_x, h * NT + (n + 1))
                        if n == 0:
                            dve.wait_ge(df_cs, h * 128 + 32)
                            nc.vector.tensor_tensor(ring[:, 2, :], ring[:, 0, :], cos_c, ALU.mult).then_inc(df_t1, 1)
                            for m in range(2):
                                nc.vector.memset(df_m[m][96:P, :].bitcast(F32), 0.0).then_inc(df_rows0, 1)
                    if n >= 1:
                        df_rotate(h, n - 1)
                        if n < NT:
                            dve.wait_ge(df_cs, h * 128 + 32 * (n + 1))
                            nc.vector.tensor_tensor(ring[:, 2 + n % 2, :], ring[:, n % 2, :], cos_c, ALU.mult).then_inc(df_t1, 1)
                dve.wait_ge(df_lo, h * NT + NT)
                for what, k in DF_ORDER[final]:
                    if what == "u":
                        df_unit(h, k)
                    if what == "s" and not final and 9 <= k < 9 + DC:
                        split_lo(h + (C_DF + 1), NARROW, k - 9)
                    if what == "f":
                        df_end(h, k)
                    if what == "g":
                        df_norm(h, k)
                    if what == "w":
                        dve.wait_ge(wo_hi_ok, k + 1)
                        nc.vector.tensor_tensor(wo_lo[:, k, :], w_raw[:, (k % 2) * D:(k % 2 + 1) * D], wo_hi[:, k, :].bitcast(F32),
                                                ALU.subtract).then_inc(wo_lo_ok, 1)

            for m in range(2):
                nc.vector.memset(df_s[m][96:P, :].bitcast(F32), 0.0).then_inc(df_set, 1)
            nc.vector.memset(nm_win[:].bitcast(F32), 0.0).then_inc(df_set, 1)
            dve.wait_ge(df_set, 3)
            for m in range(2):
                e = nc.vector.memset(df_s[m][96:97, :].bitcast(F32), 1.0)
            e.then_inc(df_set, 1)
            with dve.Fori(0, DF_H - 1) as h:
                differential(h, False)
            differential(DF_H - 1, True)

            def out_gate(t, u, value):
                dve.wait_ge(o_in[u], value)
                nc.vector.tensor_tensor(yb[:, u, :], yb[:, u, :], gb[:, u, :], ALU.mult).then_inc(o_yg, 1)

            def out_lo(t, u):
                for g in range(2):
                    dve.wait_ge(o_thi, t * 2 + (g + 1))
                    nc.vector.tensor_tensor(yt_lo[:, u, 4 * g:4 * g + 4, :], ps[:, 2 * u + g, :].rearrange("p (c s) -> p c s", c=4),
                                            yt_hi[:, u, 4 * g:4 * g + 4, :].bitcast(F32), ALU.subtract).then_inc(o_tlo, 1)

            def out_norm(t, u, value):
                dve.wait_ge(o_sq, t * 2 + 2)
                nc.vector.tensor_tensor(col(5, u), col(0, u), col(1, u), ALU.add).then_inc(o_ch, 1)
                dve.wait_ge(o_ch, t + 1)
                nc.vector.tensor_scalar(col(2, u), col(5, u), 1.0 / D, EPS, ALU.mult, ALU.add).then_inc(o_var, 1)
                dve.wait_ge(o_y0, t + 1)
                newton(col(2, u), col(4, u), col(5, u), small[:, 4 + u:5 + u], o_nr, t * 4)
                for g in range(2):
                    cols = slice(g * 512, (g + 1) * 512)
                    nc.vector.scalar_tensor_tensor(out=ob[:, u, cols], in0=ps[:, 4 + 2 * u + g, :], scalar=small[:, 4 + u:5 + u],
                                                   in1=gpost_b[:, cols], op0=ALU.mult, op1=ALU.mult).then_inc(o_n, 1)
                dve.wait_ge(o_n, t * 2 + 2)
                dve.wait_ge(o_xr[u], value)
                nc.vector.tensor_tensor(ob[:, u, :], ob[:, u, :], xr[:, u, :], ALU.add).then_inc(o_fin, 1)

            dve.wait_ge(gpost_in, 16)
            out_gate(0, 0, 32)
            out_gate(1, 1, 32)
            out_lo(0, 0)
            out_lo(1, 1)
            out_gate(2, 0, 64)
            out_norm(0, 0, 16)
            out_lo(2, 0)
            out_gate(3, 1, 64)
            out_norm(1, 1, 16)
            with dve.Fori(0, SB // 2 - 2) as i:
                for u in range(2):
                    out_lo(i * 2 + (u + 3), 1 - u)
                    out_gate(i * 2 + (u + 4), u, i * 32 + 96)
                    out_norm(i * 2 + (u + 2), u, i * 16 + 32)
            out_lo(SB - 1, 1)
            out_norm(SB - 2, 0, 16 * SB // 2)
            out_norm(SB - 1, 1, 16 * SB // 2)

        @block.gpsimd
        def _(pool):
            with pool.Fori(0, SB_H) as h:
                for i in range(N_ST):
                    j0 = SB_STEPS[i][2]
                    pool.wait_ge(sb_e, h * N_ST + (i + 1))
                    pool.sem_inc(pool_go, 1)
                    e = ring[:, i % 3, j0 * P:]
                    nc.gpsimd.tensor_scalar(e, e, E_MAX, 0.0, ALU.min, ALU.max).then_inc(sb_clamp, 1)

            def differential(h):
                for n in range(NT):
                    cols = slice(n * TQ, (n + 1) * TQ)
                    pool.wait_ge(df_lo, h * NT + (n + 1))
                    for m in range(2):
                        for k, (dst, q0, src) in enumerate(((df_s, DQ, 2 * DQ + m * DQ), (df_m, 2 * DQ, m * DQ))):
                            pool.wait_ge(df_pl_p, 1 + h * 16 + (4 * n + 2 * m + k))
                            pool.sem_inc(pool_go, 1)
                            nc.gpsimd.tensor_scalar(dst[m][q0:q0 + DQ, cols], lo_tmp[src:src + DQ, n % 2, :].bitcast(F32),
                                                    1.0, 0.0, ALU.mult, ALU.add).then_inc(df_pl_p, 1)

            with pool.Fori(0, DF_H) as h:
                differential(h)

            pool.wait_ge(df_t2, 1 + DF_H * NT)
            pool.wait_ge(w_lo_ok, (C_DF + DF_H) * DC)
            for dc in range(DC):
                if dc >= 2:
                    pool.wait_ge(wo_lo_ok, dc - 1)
                nc.gpsimd.dma_start(w_raw[:, (dc % 2) * D:(dc % 2 + 1) * D], w_out[dc * P:(dc + 1) * P, :]).then_inc(wo_in[dc % 2], 16)


def kernel(x, mem, positions, w_in, w_mem_kv, w_out, g_pre, g_post, g_mem, g_subln, df_lambda):
    import concourse.bacc as bacc
    from concourse.bass_utils import run_bass_kernel_spmd

    def tiled(cols):
        return np.ascontiguousarray(cols.reshape(DC, P, -1).transpose(1, 0, 2).reshape(P, -1))

    w = np.asarray(w_in)[0]
    names = ("sb_q", "sb_k", "sb_v", "sb_g", "df_q", "df_k", "df_v", "df_g", "m_q", "m_g")
    sizes = (512, 512, 512, 512, 256, 256, 256, 256, 256, 256)
    part, at = {}, 0
    for name, n in zip(names, sizes):
        part[name] = w[:, at:at + n]
        at += n
    wide = np.concatenate([part[n] for n in ("sb_v", "df_v", "sb_g", "df_g", "m_g")], axis=1)
    wide = np.stack([tiled(wide[:, c * WIDE:(c + 1) * WIDE]) for c in range(N_V + N_G)])
    kv = np.asarray(w_mem_kv)[0]

    def head(q, k, h):
        return np.concatenate([part[q][:, h * HD:(h + 1) * HD], part[k][:, h * HD:(h + 1) * HD]], axis=1)

    narrow = [head("sb_q", "sb_k", h) for h in range(SB_H)]
    narrow += [kv[:, c * P:(c + 1) * P] for c in range(4)]
    narrow += [part["m_q"][:, c * P:(c + 1) * P] for c in range(2)]
    narrow += [head("df_q", "df_k", h) for h in range(DF_H)]
    narrow = np.stack([tiled(c) for c in narrow])

    r = np.arange(P)
    rot = np.zeros((P, P), np.float32)
    for g in range(0, P, DQ):
        for j in range(4):
            rot[g + 4 + j, g + j] = -1.0
            rot[g + j, g + 4 + j] = 1.0
    late = (r[:, None] >= 64) & (r[None, :] < 64)
    const_sq = np.stack([
        np.eye(P), -(r[:, None] >= r[None, :]).astype(np.float32), rot,
        NEG * (r[:, None] >= r[None, :]), NEG * late, NEG * late.T]).astype(np.float32)
    inv = np.float32(1.0) / (np.float32(THETA) ** (np.arange(0, 8, 2, dtype=np.float32) / np.float32(8)))
    const_col = np.zeros((P, 1), np.float32)
    for g in range(0, P, DQ):
        const_col[g:g + 4, 0] = inv
        const_col[g + 4:g + 8, 0] = inv

    arrays = {
        "x": np.asarray(x)[0], "mem": np.asarray(mem)[0], "positions": np.asarray(positions),
        "w_wide": wide, "w_narrow": narrow, "w_out": np.asarray(w_out)[0],
        "g_pre": np.asarray(g_pre), "g_post": np.asarray(g_post), "g_mem": np.asarray(g_mem),
        "g_subln": np.asarray(g_subln), "df_lambda": np.asarray(df_lambda).reshape(1, 4 * DQ),
        "const_sq": const_sq, "const_col": const_col,
    }
    nc = bacc.Bacc("TRN2", target_bir_lowering=False, num_devices=1)
    arrays = {f"in_{n}": np.ascontiguousarray(a) for n, a in arrays.items()}
    args = [nc.dram_tensor(n, a.shape, mybir.dt.from_np(a.dtype), kind="ExternalInput").ap() for n, a in arrays.items()]
    args.append(nc.dram_tensor("out_y", (S, D), F32, kind="ExternalOutput").ap())
    build(nc, *args)
    r = run_bass_kernel_spmd(nc, [arrays], core_ids=[0])
    return r.results[0]["out_y"].reshape(1, S, D)
```

```python
from contextlib import ExitStack
import math

import numpy as np
import concourse.bass as bass
from concourse import mybir

F32 = mybir.dt.float32
F32R = mybir.dt.float32r
BF16 = mybir.dt.bfloat16
I32 = mybir.dt.int32
ACT = mybir.ActivationFunctionType
ALU = mybir.AluOpType
AXX = mybir.AxisListType.X

P = 128
D = 1024
S = 2048
DC = D // P
SB = S // P
TQ = 512
NT = S // TQ
NMEM = 256
EPS = 1e-6
HD = 64
SB_H, DF_H, M_H = 8, 4, 4
DQ = 32
V_W = (SB_H + DF_H) * HD
WIDE, NARROW = 256, 128
N_V, N_G = V_W // WIDE, D // WIDE
C_SB = N_V + N_G
C_MK = C_SB + SB_H
C_M = C_MK + 4
C_DF = C_M + M_H // 2
NEG = -1e30
Z_MAX = 44.0
THETA = 500000.0
LAMBDA_INIT = 0.8 - 0.6 * math.exp(-0.3 * 0)

SB_STEPS = [(t, kb, max(0, kb - 4 * t)) for t in range(NT) for kb in range(4 * t + 4)]
N_ST = len(SB_STEPS)
SB_LAST = {t: max(i for i, s in enumerate(SB_STEPS) if s[0] == t) for t in range(NT)}
Z_BANK = (0, 1, 2, 3, 6)
SB_LEAD = 5
SB_PROJECT = ((0, 2, 5), (0, 3, 14), (1, 0, 28), (1, 1, 36))
SB_SPLIT = 20
SB_MULS = [i for i, s in enumerate(SB_STEPS) if s[1] > 0]

DF_STEPS = [(t, kb, max(0, kb - 4 * t), m) for t in range(NT) for kb in range(4 * t + 4) for m in range(2)]
N_DF = len(DF_STEPS)
DF_UNITS = []
for _t in range(NT):
    DF_UNITS += [("max", _t, j, m, c, min(TQ, (4 * _t + j + 1) * P - c * TQ))
                 for j in range(4) for m in range(2) for c in range(_t + 1)]
    DF_UNITS += [("row", _t, 0, m, 0, 0) for m in range(2)]
N_UN = len(DF_UNITS)


def df_unit_range(t):
    idx = [u for u, x in enumerate(DF_UNITS) if x[1] == t]
    return idx[0], idx[-1] + 1


def df_project_at(n, at):
    return {at: [("P", (n, 0))], at + 1: [("P", (n, 1))], at + 2: [("P", (n, 2))], at + 3: [("P", (n, 3)), ("x", n)],
            at + 5: [("r", n)], **{at + 7 + k: [("R", (n, k))] for k in range(4)}}


DF_AT = {0: [("r", 2)], 1: [("R", (2, 0))], 2: [("R", (2, 1))], 3: [("R", (2, 2))], 4: [("R", (2, 3))],
         11: [("P", (3, 0)), ("P", (3, 1))], 12: [("P", (3, 2)), ("P", (3, 3)), ("x", 3)], 14: [("r", 3)],
         **{16 + k: [("R", (3, k))] for k in range(4)}}
DF_NEXT = df_project_at(4, 57) | df_project_at(5, 68)
DF_SPLIT = 26
PJ_BANK, EX_BANK = (4, 4, 6, 4, 4, 4), (5, 5, 7, 5, 5, 5)
X_SLOT, XC_SLOT, XR_SLOT = 5, 3, 4


def df_order(final):
    units = list(range(*df_unit_range(0)))
    out = []
    for part in range(4):
        out += [("P", (2, part))] + [("u", units.pop(0)) for _ in range(2) if part]
    out += [("x", 2)] + [("u", u) for u in units]
    step = 0
    for t in range(NT):
        n = 8 * (t + 1)
        units = list(range(*df_unit_range(t + 1))) if t + 1 < NT else []
        body, rows = units[:-2], units[-2:]
        room = max(n - 4, 1)
        for k in range(n):
            out.append(("s", step))
            take = -(-len(body) // max(room - k, 1)) if body else 0
            out += [("u", body.pop(0)) for _ in range(min(take, len(body)))]
            if k == n - 2:
                out += [("u", r) for r in rows]
            if step:
                out.append(("p", step - 1))
            out += DF_AT.get(step, []) + (DF_NEXT.get(step, []) if not final else [])
            if t:
                out += [(e, t - 1) for e, at in (("f", 1), ("l", 3), ("g", 5)) if k == at]
            if final and t == NT - 1 and k >= 8 and k % 3 == 2:
                out.append(("w", (k - 8) // 3))
            step += 1
    return out + [("p", step - 1), ("f", NT - 1), ("l", NT - 1), ("g", NT - 1)]


DF_START = [e for n in range(2) for e in [("P", (n, p)) for p in range(4)] + [("x", n), ("r", n)] + [("R", (n, k)) for k in range(4)]]
DF_ORDER = {final: df_order(final) for final in (False, True)}


def build(nc, x, mem, positions, w_wide, w_narrow, w_out, g_pre, g_post, g_mem, g_subln,
          df_lambda, const_sq, const_col, out):
    ctx = ExitStack()
    with ctx:
        def sb(name, shape, dt, stack=ctx):
            return stack.enter_context(nc.sbuf_tensor(name, shape, dt))

        def sem(name):
            return ctx.enter_context(nc.semaphore(name))

        def dram(name, shape):
            return nc.dram_tensor(name, shape, F32, kind="Internal").ap()

        v_scr = dram("v_scr", (SB_H + DF_H, S, HD))
        gate_scr = dram("gate_scr", (S, D))
        y_scr = dram("y_scr", (S, D))
        rot_scr = dram("rot_scr", (2, P, S))

        ident = sb("ident", [P, P], F32)
        negtri = sb("negtri", [P, P], F32R)
        rotperm = sb("rotperm", [P, P], F32)
        ident_b = sb("ident_b", [P, P], BF16)
        sb_mask = sb("sb_mask", [P, P], BF16)
        df_mask_kq = sb("df_mask_kq", [P, P], BF16)
        df_mask_qk = sb("df_mask_qk", [P, P], BF16)
        small = sb("small", [P, 256], F32)
        invf = small[:, 0:1]
        lam = small[:, 1:2]
        ident_r = sb("ident_r", [P, P], F32R)
        w_raw = sb("w_raw", [P, DC * WIDE], F32)
        w_hl = sb("w_hl", [P, 2 * DC * WIDE], F32R)
        with ExitStack() as a:
            ring_r = sb("ring_r", [P, 6, TQ], F32R, a)
        ring = sb("ring", [P, 6, TQ], F32)
        v1 = sb("v1", [P, SB, HD + 1], F32)
        acc = sb("acc", [P, 2, 4, HD], F32)
        ps = ctx.enter_context(nc.psum_tensor("ps", [P, 8, 512], F32))

        with ExitStack() as first:
            ht_hi = sb("ht_hi", [P, DC, S], F32R, first)
            ht_lo = sb("ht_lo", [P, DC, S], F32R, first)
            with ExitStack() as a:
                xb = sb("xb", [P, 2, D], F32, a)
                hb = sb("hb", [P, 2, D], F32, a)
                gpre_b = sb("gpre_b", [P, D], F32, a)
                cst = sb("cst", [P, 6, P], F32, a)
            with ExitStack() as a:
                ang = sb("ang", [P, S], F32, a)
                turns = sb("turns", [P, S], F32, a)
                red = sb("red", [P, S], F32, a)
                trig = sb("trig", [P, S], F32, a)
            with ExitStack() as a:
                sb_s = sb("sb_s", [P, S], F32R, a)
                sb_ma = sb("sb_ma", [P, S], F32R, a)
                sb_mb = sb("sb_mb", [P, S], F32R, a)
                sp_hi = sb("sp_hi", [P, 4, TQ], F32R, a)
            with ExitStack() as a:
                km_hi = sb("km_hi", [P, 2, NMEM], F32R, a)
                km_lo = sb("km_lo", [P, 2, NMEM], F32R, a)
                vm = sb("vm", [P, 2, M_H * HD], F32, a)
                with ExitStack() as b:
                    mt_hi = sb("mt_hi", [P, DC, NMEM], F32R, b)
                    mt_lo = sb("mt_lo", [P, DC, NMEM], F32R, b)
                with ExitStack() as b:
                    qm_hi = sb("qm_hi", [P, S], F32R, b)
                    qm_lo = sb("qm_lo", [P, S], F32R, b)
            with ExitStack() as a:
                df_s = [sb(f"df_s{m}", [P, S], F32R, a) for m in range(2)]
                df_m = [sb(f"df_m{m}", [P, S], F32R, a) for m in range(2)]
                nm_win = sb("nm_win", [P, 96 + 8], F32R, a)
        with ExitStack() as last:
            wo_hi = sb("wo_hi", [P, DC, D], F32R, last)
            wo_lo = sb("wo_lo", [P, DC, D], F32R, last)
            yt_hi = sb("yt_hi", [P, 2, DC, P], F32R, last)
            yt_lo = sb("yt_lo", [P, 2, DC, P], F32R, last)
            yb = sb("yb", [P, 2, D], F32, last)
            gb = sb("gb", [P, 2, D], F32, last)
            xr = sb("xr", [P, 2, D], F32, last)
            ob = sb("ob", [P, 2, D], F32, last)
            gpost_b = sb("gpost_b", [P, D], F32, last)

        mem_x, mem_h, mem_g = (ring[:, 2 * i:2 * i + 2, :].rearrange("p a b -> p (a b)") for i in range(3))
        gsub_b = small[:, 64:128]
        lam_in = small[:, 128:256]

        def w_hi(cols, dc):
            return w_hl[:, dc * cols:(dc + 1) * cols]

        def w_lo(cols, dc):
            return w_hl[:, (DC + dc) * cols:(DC + dc + 1) * cols]

        def raw(cols, dc):
            return w_raw[:, dc * cols:(dc + 1) * cols]

        spare = w_hl[:, 2 * DC * NARROW:].rearrange("p (a u n) -> p a u n", a=2, u=2)
        hi_tmp, lo_tmp = spare[:, 0], spare[:, 1]
        cos_c = w_raw[:, DC * NARROW:DC * NARROW + TQ]
        sin_c = w_raw[:, DC * NARROW + TQ:DC * NARROW + 2 * TQ]

        def col(k, u, n=1):
            return small[:, 8 + 8 * k + 4 * u:8 + 8 * k + 4 * u + n]

        const_in, const_ok = sem("const_in"), sem("const_ok")
        x_in = [sem("x_in0"), sem("x_in1")]
        x_sq, x_var, x_ln, x_y0, x_nr, h_rows = (sem(n) for n in ("x_sq", "x_var", "x_ln", "x_y0", "x_nr", "h_rows"))
        ht_ps, ht_hi_ok, ht_lo_ok = sem("ht_ps"), sem("ht_hi_ok"), sem("ht_lo_ok")
        w_raw_in, w_hi_ok, w_lo_ok, w_free = sem("w_raw_in"), sem("w_hi_ok"), sem("w_lo_ok"), sem("w_free")
        vg_ps, vg_ok, vg_e, vg_ch = sem("vg_ps"), sem("vg_ok"), sem("vg_e"), sem("vg_ch")
        vg_out = [sem("vg_out0"), sem("vg_out1")]
        pos_in, trig_ch, trig_val, trig_out = sem("pos_in"), sem("trig_ch"), sem("trig_val"), sem("trig_out")
        sp_ps, sp_act, sp_dve = sem("sp_ps"), sem("sp_act"), sem("sp_dve")
        sb_z, sb_e, sb_ln, sb_sp, sb_hi, sb_lo, sb_cum, sb_w, sb_o, sb_acc, sb_ch = (
            sem("sb_" + n) for n in ("z", "e", "ln", "sp", "hi", "lo", "cum", "w", "o", "acc", "ch"))
        sb_zero = sem("sb_zero")
        sb_v, sb_yout = [sem("sb_v0"), sem("sb_v1")], [sem("sb_yout0"), sem("sb_yout1")]
        mm_in, mm_sq, mm_ch, mm_ln, mm_y0, mm_h, mm_ps, mm_hi, mm_lo, mm_kv, mm_ka, mm_kd = (
            sem("mm_" + n) for n in ("in", "sq", "ch", "ln", "y0", "h", "ps", "hi", "lo", "kv", "ka", "kd"))
        m_pj, m_qhi, m_qlo = sem("m_pj"), sem("m_qhi"), sem("m_qlo")
        m_s, m_mx, m_nm, m_p, m_t, m_pt, m_o, m_rc, m_y = (
            sem("m_" + n) for n in ("s", "mx", "nm", "p", "t", "pt", "o", "rc", "y"))
        m_yout = [sem("m_yout0"), sem("m_yout1")]
        df_cs, df_pj, df_x, df_px, df_t1, df_t2, df_x2, df_hi, df_lo = (
            sem("df_" + n) for n in ("cs", "pj", "x", "px", "t1", "t2", "x2", "hi", "lo"))
        df_pl_a, df_pl_d, df_pl_p, df_set = (
            sem("df_" + n) for n in ("pl_a", "pl_d", "pl_p", "set"))
        df_ups, df_mx, df_cb, df_nm = (sem("df_" + n) for n in ("ups", "mx", "cb", "nm"))
        df_z, df_e, df_o, df_fin, df_fch, df_var, df_ln, df_y0, df_gch, df_yok = (
            sem("df_" + n) for n in ("z", "e", "o", "fin", "fch", "var", "ln", "y0", "gch", "yok"))
        df_win = sem("df_win")
        df_v = [sem("df_v0"), sem("df_v1")]
        df_yout = [sem("df_yout0"), sem("df_yout1")]
        pool_go = sem("pool_go")
        lam_ch, lam_e = sem("lam_ch"), sem("lam_e")
        wo_in, wo_hi_ok, wo_lo_ok, gpost_in = [sem("wo_in0"), sem("wo_in1")], sem("wo_hi_ok"), sem("wo_lo_ok"), sem("gpost_in")
        o_in, o_xr, o_out = ([sem(f"o_{n}{u}") for u in range(2)] for n in ("in", "xr", "out"))
        o_yg, o_tps, o_thi, o_tlo, o_ps, o_sq, o_ch, o_var, o_ln, o_y0, o_nr, o_n, o_fin = (
            sem("o_" + n) for n in ("yg", "tps", "thi", "tlo", "ps", "sq", "ch", "var", "ln", "y0", "nr", "n", "fin"))

        block = ctx.enter_context(nc.Block())

        y_rows = y_scr.rearrange("(t j p) n -> t p j n", j=4, p=P)
        v_rows = v_scr.rearrange("h (b p) d -> h p b d", p=P)
        w_raw_n = w_raw[:, 0:DC * NARROW]

        @block.sync
        def _(sp):
            for one in (ht_ps, *vg_out, sb_o, sb_acc, *sb_yout, df_t1, df_t2, df_o, df_mx, df_fin, *df_yout, df_pl_p):
                sp.sem_inc(one, 1)
            sp.dma_start(cst[:], const_sq.rearrange("c p q -> p c q")).then_inc(const_in, 16)
            sp.dma_start(small[:, 0:1], const_col).then_inc(const_in, 16)
            sp.dma_start(gpre_b[:], g_pre.broadcast_to((P, D))).then_inc(const_in, 16)
            sp.dma_start(gsub_b, g_subln.broadcast_to((P, HD))).then_inc(const_in, 16)
            sp.dma_start(lam_in, df_lambda.broadcast_to((P, 4 * DQ))).then_inc(const_in, 16)

            def load_x(t, u):
                sp.dma_start(xb[:, u, :], x[bass.ts(t, P), :]).then_inc(x_in[u], 16)

            load_x(0, 0)
            load_x(1, 1)
            sp.dma_start(w_raw[:], w_wide[0]).then_inc(w_raw_in, 16)
            with sp.Fori(0, SB // 2 - 1) as i:
                for u in range(2):
                    sp.wait_ge(h_rows, i * 2 + (u + 1))
                    load_x(i * 2 + (u + 2), u)

            sp.wait_ge(h_rows, SB)
            sp.wait_ge(ht_ps, 1 + SB)
            sp.wait_ge(const_ok, 8)
            sp.dma_start(red[:].bitcast(I32), positions.broadcast_to((P, S))).then_inc(pos_in, 16)
            with sp.Fori(0, N_V) as c:
                sp.wait_ge(w_lo_ok, c * DC + DC)
                sp.dma_start(w_raw[:], w_wide[c + 1]).then_inc(w_raw_in, 16)
                for b in range(8):
                    sp.wait_ge(vg_ok, c * 8 + (8 + b + 1))
                    for r in range(2):
                        sp.dma_start(v_rows[bass.ds(c * 4, 4), :, 2 * b + r, :].rearrange("h p d -> p h d"),
                                     ring[:, b % 2, r * WIDE:(r + 1) * WIDE].rearrange("p (h d) -> p h d", h=4)
                                     ).then_inc(vg_out[b % 2], 16)

            def store_gates(c):
                for b in range(8):
                    sp.wait_ge(vg_ok, c * 8 + (N_V * 8 + 8 + b + 1))
                    for r in range(2):
                        s = (2 * b + r) * P
                        sp.dma_start(gate_scr[s:s + P, bass.ts(c, WIDE)],
                                     ring[:, b % 2, r * WIDE:(r + 1) * WIDE]).then_inc(vg_out[b % 2], 16)

            with sp.Fori(0, N_G - 1) as c:
                sp.wait_ge(w_lo_ok, c * DC + (N_V + 1) * DC)
                sp.dma_start(w_raw[:], w_wide[c + (N_V + 1)]).then_inc(w_raw_in, 16)
                store_gates(c)
            sp.wait_ge(w_lo_ok, C_SB * DC)
            sp.dma_start(w_raw_n, w_narrow[0]).then_inc(w_raw_in, 16)
            sp.wait_ge(trig_val, 2)
            sp.dma_start(rot_scr[0], turns[:]).then_inc(trig_out, 16)
            sp.dma_start(rot_scr[1], trig[:]).then_inc(trig_out, 16)
            store_gates(N_G - 1)
            for q in range(2):
                sp.wait_ge(vg_out[q], 1 + 32 * 4 * (N_V + N_G))
            sp.wait_ge(trig_out, 32)

            def load_v(h, first, end):
                sp.dma_start(v1[:, first:end, 0:HD], v_rows[h][:, first:end, :]).then_inc(sb_v[first > 0], 16)

            def stick(h, more):
                sp.wait_ge(w_lo_ok, h * DC + (C_SB + 1) * DC)
                sp.dma_start(w_raw_n, w_narrow[h + 1]).then_inc(w_raw_in, 16)
                for t in range(NT):
                    if t == NT - 1 and more:
                        sp.wait_ge(sb_o, h * N_ST + (1 + SB_STEPS.index((NT - 1, 4, 0))))
                        load_v(h + 1, 0, 4)
                        sp.wait_ge(sb_o, h * N_ST + (1 + N_ST))
                        load_v(h + 1, 4, SB)
                    sp.wait_ge(sb_acc, 1 + h * N_ST + (SB_LAST[t] + 1))
                    sp.dma_start(y_rows[t][:, :, bass.ts(h, HD)], acc[:, t % 2]).then_inc(sb_yout[t % 2], 16)

            load_v(0, 0, 4)
            load_v(0, 4, SB)
            with sp.Fori(0, SB_H - 1) as h:
                stick(h, True)
            stick(SB_H - 1, False)

            sp.wait_ge(sb_acc, 1 + SB_H * N_ST)
            sp.dma_start(mem_g, g_mem.broadcast_to((P, D))).then_inc(mm_in, 16)
            sp.dma_start(mem_x, mem[0:P, :]).then_inc(mm_in, 16)
            sp.wait_ge(mm_h, 1)
            sp.dma_start(mem_x, mem[P:2 * P, :]).then_inc(mm_in, 16)
            for c in range(C_MK, C_M):
                sp.wait_ge(w_lo_ok, (c + 1) * DC)
                sp.dma_start(w_raw_n, w_narrow[c + 1 - C_SB]).then_inc(w_raw_in, 16)
            for p in range(2):
                sp.wait_ge(w_lo_ok, (C_M + p + 1) * DC)
                sp.dma_start(w_raw_n, w_narrow[C_M + p + 1 - C_SB]).then_inc(w_raw_in, 16)
                for qb in range(SB):
                    sp.wait_ge(m_y, p * SB + qb + 1)
                    c0 = (SB_H + DF_H + 2 * p) * HD
                    sp.dma_start(y_scr[qb * P:(qb + 1) * P, c0:c0 + 2 * HD].rearrange("p (a d) -> p a d", a=2),
                                 acc[:, qb % 2, 0:2, :]).then_inc(m_yout[qb % 2], 16)

            def load_cos_sin(h, n):
                sp.wait_ge(df_t1, 1 + h * NT + n)
                sp.wait_ge(df_t2, 1 + h * NT + n)
                for q, dst in enumerate((cos_c, sin_c)):
                    sp.dma_start(dst, rot_scr[q, :, n % NT * TQ:(n % NT + 1) * TQ]).then_inc(df_cs, 16)

            def load_df_v(h, first, end):
                sp.dma_start(v1[:, first:end, 0:HD], v_rows[h + SB_H][:, first:end, :]).then_inc(df_v[first > 0], 16)

            def differential(h, more):
                load_cos_sin(h, 2)
                load_cos_sin(h, 3)
                if more:
                    sp.wait_ge(w_lo_ok, h * DC + (C_DF + 1) * DC)
                    sp.dma_start(w_raw_n, w_narrow[h + (C_DF + 1 - C_SB)]).then_inc(w_raw_in, 16)
                for t in range(NT):
                    if t == NT - 1 and more:
                        sp.wait_ge(df_o, 1 + h * N_DF + DF_STEPS.index((NT - 1, 4, 0, 0)))
                        load_df_v(h + 1, 0, 4)
                        load_cos_sin(h, 4)
                        load_cos_sin(h, 5)
                        sp.wait_ge(df_o, 1 + h * N_DF + N_DF)
                        load_df_v(h + 1, 4, SB)
                    sp.wait_ge(df_yok, h * NT + (t + 1))
                    sp.dma_start(y_rows[t][:, :, bass.ds(h * HD + SB_H * HD, HD)], acc[:, t % 2]).then_inc(df_yout[t % 2], 16)

            load_cos_sin(0, 0)
            load_df_v(0, 0, 4)
            load_df_v(0, 4, SB)
            load_cos_sin(0, 1)
            with sp.Fori(0, DF_H - 1) as h:
                differential(h, True)
            differential(DF_H - 1, False)

            for q in range(2):
                sp.wait_ge(sb_yout[q], 1 + 16 * SB_H * NT // 2)
                sp.wait_ge(m_yout[q], 16 * SB)
                sp.wait_ge(df_yout[q], 1 + 16 * DF_H * NT // 2)

            def load_y(t, u):
                sp.dma_start(yb[:, u, :], y_scr[bass.ts(t, P), :]).then_inc(o_in[u], 16)
                sp.dma_start(gb[:, u, :], gate_scr[bass.ts(t, P), :]).then_inc(o_in[u], 16)

            def load_xr(t, u):
                sp.dma_start(xr[:, u, :], x[bass.ts(t, P), :]).then_inc(o_xr[u], 16)

            def store(t, u):
                sp.wait_ge(o_fin, t + 1)
                sp.dma_start(out[bass.ts(t, P), :], ob[:, u, :]).then_inc(o_out[u], 16)

            for u in range(2):
                load_y(u, u)
                load_xr(u, u)
            sp.dma_start(gpost_b[:], g_post.broadcast_to((P, D))).then_inc(gpost_in, 16)
            with sp.Fori(0, SB // 2 - 1) as i:
                for u in range(2):
                    sp.wait_ge(o_tps, i * 2 + (u + 1))
                    load_y(i * 2 + (u + 2), u)
                    store(i * 2 + u, u)
                    load_xr(i * 2 + (u + 2), u)
            for u in range(2):
                store(SB - 2 + u, u)
            for u in range(2):
                sp.wait_ge(o_out[u], 16 * SB // 2)

        @block.tensor
        def _(pe):
            pe.wait_ge(const_ok, 8)

            def transposes(t, u, free):
                pe.wait_ge(h_rows, t + 1)
                for dc in range(DC):
                    if dc % 4 == 0 and free is not None:
                        pe.wait_ge(ht_lo_ok, free + (dc // 4 + 1))
                    mm = pe.transpose(ps[:, 2 * u + dc // 4, (dc % 4) * P:(dc % 4 + 1) * P],
                                      hb[:, u, dc * P:(dc + 1) * P], ident[:])
                mm.then_inc(ht_ps, 1)

            transposes(0, 0, None)
            transposes(1, 1, None)
            with pe.Fori(0, SB // 2 - 1) as i:
                for u in range(2):
                    transposes(i * 2 + (u + 2), u, i * 4 + 2 * u)

            pe.wait_ge(ht_lo_ok, 2 * SB)
            with pe.Fori(0, N_V + N_G) as c:
                for b in range(8):
                    pe.wait_ge(vg_ok, c * 8 + (b + 1))
                    for r in range(2):
                        s = (2 * b + r) * P
                        dst = ps[:, b, r * WIDE:(r + 1) * WIDE]
                        for dc in range(DC):
                            if b == 0 and r == 0:
                                pe.wait_ge(w_lo_ok, c * DC + (dc + 1))
                            pe.matmul(dst, ht_hi[:, dc, s:s + P], w_hi(WIDE, dc), start=(dc == 0), stop=False)
                            pe.matmul(dst, ht_hi[:, dc, s:s + P], w_lo(WIDE, dc), start=False, stop=False)
                            mm = pe.matmul(dst, ht_lo[:, dc, s:s + P], w_hi(WIDE, dc), start=False, stop=(dc == DC - 1))
                            if b == 7 and r == 1 and dc < DC - 1:
                                mm.then_inc(w_free, 1)
                    mm.then_inc(vg_ps, 1)

            def project(c, n, bank, done, part=None):
                for dc in range(DC) if part is None else range(2 * part, 2 * part + 2):
                    if n == 0:
                        pe.wait_ge(w_lo_ok, c * DC + (dc + 1))
                    cols = slice(n * TQ, (n + 1) * TQ)
                    pe.matmul(ps[:, bank, :], w_hi(NARROW, dc), ht_hi[:, dc, cols], start=(dc == 0), stop=False)
                    pe.matmul(ps[:, bank, :], w_hi(NARROW, dc), ht_lo[:, dc, cols], start=False, stop=False)
                    mm = pe.matmul(ps[:, bank, :], w_lo(NARROW, dc), ht_hi[:, dc, cols], start=False, stop=(dc == DC - 1))
                    if n == NT - 1 and dc < DC - 1:
                        mm.then_inc(w_free, 1)
                if part in (None, 3):
                    mm.then_inc(done, 1)

            def sb_scores(h, i):
                t, kb, j0 = SB_STEPS[i % N_ST]
                if kb == 0:
                    n = i // N_ST * NT + t + 1
                    pe.wait_ge(sp_act, h * 12 + 3 * n)
                    pe.wait_ge(sp_dve, h * 8 + 2 * n)
                if i >= 5:
                    pe.wait_ge(sb_w, h * N_ST + (i - 4))
                z = ps[:, Z_BANK[i % 5], j0 * P:TQ]
                cols = slice(t * TQ + j0 * P, (t + 1) * TQ)
                diag = kb >= 4 * t
                pe.matmul(z, sb_s[:, kb * P:(kb + 1) * P], sb_ma[:, cols], start=True, stop=False)
                mm = pe.matmul(z, sb_s[:, kb * P:(kb + 1) * P], sb_mb[:, cols], start=False, stop=True)
                if diag:
                    mm = pe.matmul(ps[:, Z_BANK[i % 5], j0 * P:(j0 + 1) * P], ident_b[:], sb_mask[:], start=False, stop=True,
                                   skip_group_check=True)
                mm.then_inc(sb_z, 1)

            def sb_sums(h, i):
                j0 = SB_STEPS[i % N_ST][2]
                pe.wait_ge(sb_lo, h * N_ST + (i + 1))
                for part in (sp_hi, ring_r):
                    mm = pe.matmul(ps[:, Z_BANK[i % 5], j0 * P:TQ], negtri[:], part[:, i % 4, j0 * P:TQ], start=False, stop=True,
                                   skip_group_check=True)
                mm.then_inc(sb_cum, 1)

            def sb_values(h, i):
                t, kb, j0 = SB_STEPS[i % N_ST]
                if i % N_ST == 0:
                    pe.wait_ge(sb_v[0], h * 16 + (16 * (i // N_ST) + 16))
                if i == SB_STEPS.index((1, 4, 0)):
                    pe.wait_ge(sb_v[1], h * 16 + 16)
                pe.wait_ge(sb_acc, 1 + h * N_ST + max(0, i - 1))
                pe.wait_ge(sb_w, h * N_ST + (i + 1))
                for j in range(j0, 4):
                    mm = pe.matmul(ps[:, 4 + i % 2, j * (HD + 1):(j + 1) * (HD + 1)], ring[:, 4 + i % 2, j * P:(j + 1) * P],
                                   v1[:, kb, :], start=True, stop=True)
                mm.then_inc(sb_o, 1)

            pe.wait_ge(vg_ok, 8 * (N_V + N_G + 1))

            def sb_slot(h, i, more):
                for ahead, n, at in SB_PROJECT:
                    if at <= i < at + 4 and (more or not ahead):
                        if i == at:
                            k = ahead * NT + n
                            pe.wait_ge(sp_act, h * 12 + 3 * k)
                            pe.wait_ge(sp_dve, h * 8 + 2 * k)
                        project(h + (C_SB + ahead), n, 7, sp_ps, i - at)
                if more or i < N_ST:
                    sb_scores(h, i)
                if 3 <= i and (more or i < N_ST + 3):
                    sb_sums(h, i - 3)
                if 4 <= i and (more or i < N_ST + 4):
                    sb_values(h, i - 4)

            for n in range(2):
                if n:
                    pe.wait_ge(sp_act, 3)
                    pe.wait_ge(sp_dve, 2)
                project(C_SB, n, 7, sp_ps)
            pe.wait_ge(sb_zero, 1)
            for i in range(SB_LEAD):
                sb_slot(0, i, True)
            with pe.Fori(0, SB_H - 1) as h:
                for i in range(SB_LEAD, SB_LEAD + N_ST):
                    sb_slot(h, i, True)
            for i in range(SB_LEAD, SB_LEAD + N_ST):
                sb_slot(SB_H - 1, i, False)

            for b in range(2):
                pe.wait_ge(mm_h, b + 1)
                for dc in range(DC):
                    if dc % 4 == 0 and b == 1:
                        pe.wait_ge(mm_lo, dc // 4 + 1)
                    mm = pe.transpose(ps[:, dc // 4, (dc % 4) * P:(dc % 4 + 1) * P], mem_h[:, dc * P:(dc + 1) * P], ident[:])
                mm.then_inc(mm_ps, 1)
            pe.wait_ge(mm_lo, 4)
            for k in range(4):
                if k >= 2:
                    pe.wait_ge(mm_ka, k - 1)
                    pe.wait_ge(mm_kd, 2)
                for dc in range(DC):
                    pe.wait_ge(w_lo_ok, (C_MK + k) * DC + dc + 1)
                    for b in range(2 if k >= 2 else 1):
                        first, end = dc == 0, dc == DC - 1
                        if k < 2:
                            dst, rows = ps[:, 2 + k, 0:NMEM], slice(0, NMEM)
                            pe.matmul(dst, w_hi(NARROW, dc), mt_hi[:, dc, rows], start=first, stop=False)
                            pe.matmul(dst, w_hi(NARROW, dc), mt_lo[:, dc, rows], start=False, stop=False)
                            mm = pe.matmul(dst, w_lo(NARROW, dc), mt_hi[:, dc, rows], start=False, stop=end)
                        else:
                            dst, rows = ps[:, 2 * k + b, 0:P], slice(b * P, (b + 1) * P)
                            pe.matmul(dst, mt_hi[:, dc, rows], w_hi(NARROW, dc), start=first, stop=False)
                            pe.matmul(dst, mt_hi[:, dc, rows], w_lo(NARROW, dc), start=False, stop=False)
                            mm = pe.matmul(dst, mt_lo[:, dc, rows], w_hi(NARROW, dc), start=False, stop=end)
                    if dc < DC - 1:
                        mm.then_inc(w_free, 1)
                mm.then_inc(mm_kv, 1)

            for p in range(2):
                if p == 0:
                    pe.wait_ge(mm_ka, 4)
                for n in range(NT):
                    if n < 2:
                        pe.wait_ge(m_y, p * SB)
                    if n >= 2:
                        pe.wait_ge(m_qlo, p * NT + n - 1)
                    project(C_M + p, n, 6 + n % 2, m_pj)
                for i in range(SB + 2):
                    if i < SB:
                        if i % 4 == 0:
                            pe.wait_ge(m_qlo, p * NT + i // 4 + 1)
                        pe.wait_ge(m_p, max(0, p * SB + i - 1))
                        cols = slice(i * P, (i + 1) * P)
                        for a in range(2):
                            dst, half = ps[:, 2 * (i % 2) + a, 0:NMEM], slice(a * HD, (a + 1) * HD)
                            pe.matmul(dst, qm_hi[half, cols], km_hi[half, p, :], start=True, stop=False)
                            pe.matmul(dst, qm_hi[half, cols], km_lo[half, p, :], start=False, stop=False)
                            mm = pe.matmul(dst, qm_lo[half, cols], km_hi[half, p, :], start=False, stop=True)
                        mm.then_inc(m_s, 1)
                    if 1 <= i <= SB:
                        k = i - 1
                        pe.wait_ge(m_pt, max(0, p * SB + k - 1))
                        pe.wait_ge(m_p, p * SB + k + 1)
                        for ab in range(4):
                            mm = pe.transpose(ps[:, 4 + k % 2, ab * P:(ab + 1) * P], ring[:, k % 2, ab * P:(ab + 1) * P], ident[:])
                        mm.then_inc(m_t, 1)
                    if i >= 2:
                        k = i - 2
                        pe.wait_ge(m_y, max(0, p * SB + k - 1))
                        pe.wait_ge(m_pt, p * SB + k + 1)
                        for a in range(2):
                            for b in range(2):
                                mm = pe.matmul(ps[:, 6 + k % 2, a * HD:(a + 1) * HD], ring[:, 2 + k % 2, (2 * a + b) * P:(2 * a + b + 1) * P],
                                               vm[:, b, (2 * p + a) * HD:(2 * p + a + 1) * HD], start=(b == 0), stop=(b == 1))
                        mm.then_inc(m_o, 1)

            def df_unit(h, u):
                kind, t, j, m, c, w = DF_UNITS[u]
                bank = 2 + u % 2
                pe.wait_ge(df_mx, 1 + h * N_UN + max(0, u - 1))
                if kind == "row":
                    pe.wait_ge(df_nm, h * NT + (t + 1))
                    for j in range(4):
                        mm = pe.matmul(ps[0:97, bank, j * P:(j + 1) * P], nm_win[:, m * 4 + j:m * 4 + j + 97], ident_r[:],
                                       start=True, stop=True)
                    mm.then_inc(df_ups, 1)
                    return
                if (j, m, c) == (0, 0, 0):
                    pe.wait_ge(df_pl_a, h * 16 + 4 * (t + 1))
                    pe.wait_ge(df_pl_d, h * 16 + 4 * (t + 1))
                    pe.wait_ge(df_pl_p, 1 + h * 24 + 6 * (t + 1))
                qb = 4 * t + j
                mm = pe.matmul(ps[:, bank, 0:w], df_m[m][:, qb * P:(qb + 1) * P], df_s[m][:, c * TQ:c * TQ + w],
                               start=True, stop=True)
                if c == t:
                    mm = pe.matmul(ps[:, bank, j * P:(j + 1) * P], ident_b[:], df_mask_qk[:], start=False, stop=True,
                                   skip_group_check=True)
                mm.then_inc(df_ups, 1)

            def df_scores(h, i):
                t, kb, j0, m = DF_STEPS[i]
                if kb == 0 and m == 0:
                    pe.wait_ge(df_mx, 1 + h * N_UN + df_unit_range(t)[1])
                if i >= 2:
                    pe.wait_ge(df_e, h * N_DF + (i - 1))
                diag = kb >= 4 * t
                mm = pe.matmul(ps[:, i % 2, j0 * P:TQ], df_s[m][:, kb * P:(kb + 1) * P],
                               df_m[m][:, t * TQ + j0 * P:(t + 1) * TQ], start=True, stop=True)
                if diag:
                    mm = pe.matmul(ps[:, i % 2, j0 * P:(j0 + 1) * P], ident_b[:], df_mask_kq[:], start=False, stop=True,
                                   skip_group_check=True)
                mm.then_inc(df_z, 1)

            def df_values(h, i):
                t, kb, j0, m = DF_STEPS[i]
                if i == 0:
                    pe.wait_ge(df_v[0], h * 16 + 16)
                if (t, kb, m) == (1, 4, 0):
                    pe.wait_ge(df_v[1], h * 16 + 16)
                if kb == 0 and m == 0:
                    pe.wait_ge(df_fin, 1 + h * NT + max(0, t - 1))
                    if t < 3:
                        pe.wait_ge(df_t2, 1 + h * NT + (t + 2))
                pe.wait_ge(df_e, h * N_DF + (i + 1))
                for j in range(j0, 4):
                    mm = pe.matmul(ps[:, 4 + 2 * (t % 2) + m, j * (HD + 1):(j + 1) * (HD + 1)], ring[:, i % 3, j * P:(j + 1) * P],
                                   v1[:, kb, :], start=(kb == 0 and j == 0), stop=(kb == 4 * t + j), skip_group_check=True)
                mm.then_inc(df_o, 1)

            def df_exchange(h, n):
                if n in (1, 5):
                    pe.wait_ge(df_t2, 1 + h * NT + n)
                pe.wait_ge(df_x, h * NT + (n + 1))
                pe.matmul(ps[:, EX_BANK[n], :], rotperm[:], ring[:, X_SLOT, :], start=True, stop=True).then_inc(df_px, 1)

            def df_project(h, n, part):
                if part == 0 and n in (2, 3, 4):
                    pe.wait_ge(df_fin, 1 + h * NT + (0, 1, 3)[n - 2])
                if part == 0 and n in (1, 5):
                    pe.wait_ge(df_x, h * NT + n)
                project(h + (C_DF + n // NT), n % NT, PJ_BANK[n], df_pj, part)

            def differential(h, order):
                for what, k in order:
                    if what == "u":
                        df_unit(h, k)
                    if what == "s":
                        df_scores(h, k)
                    if what == "p":
                        df_values(h, k)
                    if what == "P":
                        df_project(h, *k)
                    if what == "r":
                        df_exchange(h, k)

            pe.wait_ge(m_y, 2 * SB)
            differential(0, DF_START)
            pe.wait_ge(df_set, 6)
            with pe.Fori(0, DF_H - 1) as h:
                differential(h, DF_ORDER[False])
            differential(DF_H - 1, DF_ORDER[True])

            def out_transposes(t, u, free):
                pe.wait_ge(o_yg, t + 1)
                for dc in range(DC):
                    if dc % 4 == 0 and free is not None:
                        pe.wait_ge(o_tlo, free + (dc // 4 + 1))
                    mm = pe.transpose(ps[:, 2 * u + dc // 4, (dc % 4) * P:(dc % 4 + 1) * P],
                                      yb[:, u, dc * P:(dc + 1) * P], ident[:])
                mm.then_inc(o_tps, 1)

            def out_products(t, u, free):
                pe.wait_ge(o_tlo, t * 2 + 2)
                for g in range(2):
                    if free is not None:
                        pe.wait_ge(o_n, free + (g + 1))
                    dst, cols = ps[:, 4 + 2 * u + g, :], slice(g * 512, (g + 1) * 512)
                    for dc in range(DC):
                        pe.matmul(dst, yt_hi[:, u, dc, :], wo_hi[:, dc, cols], start=(dc == 0), stop=False)
                        pe.matmul(dst, yt_hi[:, u, dc, :], wo_lo[:, dc, cols], start=False, stop=False)
                        mm = pe.matmul(dst, yt_lo[:, u, dc, :], wo_hi[:, dc, cols], start=False, stop=(dc == DC - 1))
                    mm.then_inc(o_ps, 1)

            pe.wait_ge(df_fin, 1 + DF_H * NT)
            out_transposes(0, 0, None)
            out_transposes(1, 1, None)
            pe.wait_ge(wo_lo_ok, DC)
            out_products(0, 0, None)
            out_transposes(2, 0, 0)
            out_products(1, 1, None)
            with pe.Fori(0, SB // 2 - 2) as i:
                for u in range(2):
                    out_transposes(i * 2 + (u + 3), 1 - u, i * 4 + (2 * u + 2))
                    out_products(i * 2 + (u + 2), u, i * 4 + 2 * u)
            out_transposes(SB - 1, 1, 2 * (SB - 3))
            out_products(SB - 2, 0, 2 * (SB - 4))
            out_products(SB - 1, 1, 2 * (SB - 3))

        @block.scalar
        def _(act):
            act.preload_act_table_set("natural_log_exp_and_others")

            def split_hi(c, cols, dc, free, whole=False):
                if dc == 0:
                    act.wait_ge(w_raw_in, c * 16 + 16)
                if free is not None:
                    done, value = free
                    if dc < DC - 1 and not whole:
                        act.wait_ge(w_free, c * (DC - 1) + (dc + 1 - (DC - 1)))
                    else:
                        act.wait_ge(done, value)
                nc.scalar.activation(w_hi(cols, dc), raw(cols, dc), ACT.Copy).then_inc(w_hi_ok, 1)

            def rsqrt_of(var, ln, y0, var_ok, n, ln_ok, y0_ok):
                act.wait_ge(var_ok, n)
                nc.scalar.activation(ln, var, ACT.Ln).then_inc(ln_ok, 1)
                act.wait_ge(ln_ok, n)
                nc.scalar.activation(y0, ln, ACT.Exp, scale=-0.5).then_inc(y0_ok, 1)

            def norm_square(t, u):
                act.wait_ge(x_in[u], (t - u) * 8 + 16)
                act.wait_ge(ht_ps, 1 + t - 1) if not isinstance(t, int) or t >= 2 else None
                nc.scalar.activation(hb[:, u, :], xb[:, u, :], ACT.Square, accum_out=col(0, u)).then_inc(x_sq, 1)

            def norm_hi(t, u):
                act.wait_ge(ht_ps, 1 + t + 1)
                for g in range(2):
                    nc.scalar.activation(ht_hi[:, 4 * g:4 * g + 4, bass.ts(t, P)],
                                         ps[:, 2 * u + g, :].rearrange("p (c s) -> p c s", c=4), ACT.Copy).then_inc(ht_hi_ok, 1)

            act.wait_ge(lam_ch, 2)
            nc.scalar.activation(small[:, 2:4], small[:, 4:6], ACT.Exp).then_inc(lam_e, 1)
            norm_square(0, 0)
            rsqrt_of(col(1, 0), col(2, 0), col(3, 0), x_var, 1, x_ln, x_y0)
            for dc in range(DC):
                split_hi(0, WIDE, dc, None)
            with act.Fori(0, SB // 2 - 1) as i:
                for q in range(2):
                    u = 1 - q
                    act.wait_ge(x_in[u], i * 16 + 16 * (q + 1))
                    act.wait_ge(ht_ps, 1 + i * 2 + q)
                    nc.scalar.activation(hb[:, u, :], xb[:, u, :], ACT.Square, accum_out=col(0, u)).then_inc(x_sq, 1)
                    norm_hi(i * 2 + q, 1 - u)
                    rsqrt_of(col(1, u), col(2, u), col(3, u), x_var, i * 2 + (q + 2), x_ln, x_y0)
            act.wait_ge(x_in[1], 16 * SB // 2)
            act.wait_ge(ht_ps, 1 + SB - 2)
            nc.scalar.activation(hb[:, 1, :], xb[:, 1, :], ACT.Square, accum_out=col(0, 1)).then_inc(x_sq, 1)
            norm_hi(SB - 2, 0)
            rsqrt_of(col(1, 1), col(2, 1), col(3, 1), x_var, SB, x_ln, x_y0)
            norm_hi(SB - 1, 1)

            act.sem_inc(vg_ok, 8)
            act.wait_ge(trig_ch, 10)
            nc.scalar.activation(trig[:], red[:], ACT.Sin).then_inc(trig_val, 1)
            nc.scalar.activation(turns[:], ang[:], ACT.Sin).then_inc(trig_val, 1)
            act.preload_act_table_set("natural_log_exp_and_others")

            def vg_last(c):
                return (vg_ps, c * 8)

            with act.Fori(0, N_V) as c:
                for b in range(8):
                    if b == 7:
                        for dc in range(DC):
                            split_hi(c + 1, WIDE, dc, (vg_ps, c * 8 + 8))
                    act.wait_ge(vg_out[b % 2], 1 + c * 128 + 32 * (b // 2))
                    act.wait_ge(vg_ps, c * 8 + (b + 1))
                    nc.scalar.activation(ring[:, b % 2, :], ps[:, b, :], ACT.Copy).then_inc(vg_ok, 1)

            def gates(c, cols):
                for b in range(8):
                    if b == 7:
                        for dc in range(DC):
                            split_hi(c + (N_V + 1), cols, dc, (vg_ps, c * 8 + (N_V * 8 + 8)), whole=cols == NARROW)
                    act.wait_ge(vg_ok, c * 8 + (N_V * 8 + 8 + b - 1))
                    act.wait_ge(vg_ps, c * 8 + (N_V * 8 + b + 1))
                    nc.scalar.activation(ring[:, 2 + b % 2, :], ps[:, b, :], ACT.Exp, scale=-1.0).then_inc(vg_e, 1)

            with act.Fori(0, N_G - 1) as c:
                gates(c, WIDE)
            gates(N_G - 1, NARROW)

            def sb_exp_z(h, i):
                j0 = SB_STEPS[i % N_ST][2]
                if i >= 4:
                    act.wait_ge(sb_cum, h * N_ST + (i - 3))
                act.wait_ge(sb_z, h * N_ST + (i + 1))
                nc.scalar.activation(ring[:, i % 4, j0 * P:], ps[:, Z_BANK[i % 5], j0 * P:], ACT.Exp).then_inc(sb_e, 1)

            def sb_log(h, i):
                j0 = SB_STEPS[i % N_ST][2]
                act.wait_ge(sb_e, h * N_ST + (i + 1))
                nc.scalar.activation(ring[:, i % 4, j0 * P:], ring[:, i % 4, j0 * P:], ACT.Ln, bias=1.0).then_inc(sb_ln, 1)

            def sb_exp_w(h, i):
                j0 = SB_STEPS[i % N_ST][2]
                if i >= 2:
                    act.wait_ge(sb_o, 1 + h * N_ST + (i - 1))
                act.wait_ge(sb_cum, h * N_ST + (i + 1))
                nc.scalar.activation(ring[:, 4 + i % 2, j0 * P:], ps[:, Z_BANK[i % 5], j0 * P:], ACT.Exp).then_inc(sb_w, 1)

            def sb_stack_hi(h, n, k):
                cols = slice(n % NT * TQ, (n % NT + 1) * TQ)
                act.wait_ge(sp_ps, h * NT + (n + 1))
                dst, src, scale = ((sb_ma[0:HD, cols], ps[0:HD, 7, :], HD ** -0.5), (sb_s[HD:P, cols], ps[HD:P, 7, :], 1.0),
                                   (sb_ma[HD:P, cols], ps[0:HD, 7, :], HD ** -0.5))[k]
                nc.scalar.activation(dst, src, ACT.Copy, scale=scale).then_inc(sp_act, 1)

            def sb_slot(h, i, more):
                if 1 <= i and (more or i <= N_ST):
                    sb_log(h, i - 1)
                if more or i < N_ST:
                    sb_exp_z(h, i)
                if 3 <= i and (more or i < N_ST + 3):
                    sb_exp_w(h, i - 3)
                for ahead, n, at in SB_PROJECT:
                    if at + 4 <= i < at + 6 and (more or not ahead):
                        for k in (0, 1) if i == at + 4 else (2,):
                            sb_stack_hi(h, ahead * NT + n, k)
                if SB_SPLIT <= i < SB_SPLIT + DC:
                    split_hi(h + (C_SB + 1), NARROW, i - SB_SPLIT, (sp_ps, h * NT + NT))

            act.wait_ge(trig_out, 32)
            for q in range(2):
                act.wait_ge(vg_out[q], 1 + 32 * 4 * (N_V + N_G))
            for n in range(2):
                for k in range(3):
                    sb_stack_hi(0, n, k)
            for i in range(SB_LEAD):
                sb_slot(0, i, True)
            with act.Fori(0, SB_H - 1) as h:
                for i in range(SB_LEAD, SB_LEAD + N_ST):
                    sb_slot(h, i, True)
            for i in range(SB_LEAD, SB_LEAD + N_ST):
                sb_slot(SB_H - 1, i, False)

            for b in range(2):
                act.wait_ge(mm_in, 32 + 16 * b)
                if b:
                    act.wait_ge(mm_ps, 1)
                nc.scalar.activation(mem_h, mem_x, ACT.Square, accum_out=col(0, b)).then_inc(mm_sq, 1)
                rsqrt_of(col(1, b), col(2, b), col(3, b), mm_ch, 5 * b + 1, mm_ln, mm_y0) if b == 0 else None
                if b:
                    act.wait_ge(mm_ch, 6)
                    nc.scalar.activation(col(2, 1), col(1, 1), ACT.Ln).then_inc(mm_ln, 1)
                    act.wait_ge(mm_ln, 2)
                    nc.scalar.activation(col(3, 1), col(2, 1), ACT.Exp, scale=-0.5).then_inc(mm_y0, 1)
                act.wait_ge(mm_ps, b + 1)
                for g in range(2):
                    nc.scalar.activation(mt_hi[:, 4 * g:4 * g + 4, b * P:(b + 1) * P],
                                         ps[:, g, :].rearrange("p (c s) -> p c s", c=4), ACT.Copy).then_inc(mm_hi, 1)
            for k in range(4):
                for dc in range(DC):
                    split_hi(C_MK + k + 1, NARROW, dc, (mm_kv, k + 1))
                act.wait_ge(mm_kv, k + 1)
                if k < 2:
                    nc.scalar.activation(km_hi[:, k, :], ps[:, 2 + k, 0:NMEM], ACT.Copy).then_inc(mm_ka, 1)
                else:
                    nc.scalar.activation(vm[:, :, (k - 2) * P:(k - 1) * P], ps[:, 2 * k:2 * k + 2, 0:P], ACT.Copy).then_inc(mm_ka, 1)

            for p in range(2):
                for n in range(NT):
                    act.wait_ge(m_pj, p * NT + n + 1)
                    nc.scalar.activation(qm_hi[:, n * TQ:(n + 1) * TQ], ps[:, 6 + n % 2, :], ACT.Copy, scale=HD ** -0.5).then_inc(m_qhi, 1)
                for i in range(SB + 1):
                    if i < SB:
                        act.wait_ge(m_nm, p * SB + i + 1)
                        act.wait_ge(m_t, max(0, p * SB + i - 1))
                        act.wait_ge(m_y, max(0, p * SB + i - 1))
                        for a in range(2):
                            e = nc.scalar.activation(ring[:, i % 2, a * NMEM:(a + 1) * NMEM], ps[:, 2 * (i % 2) + a, 0:NMEM],
                                                     ACT.Exp, bias=col(1, i % 2, 2)[:, a:a + 1], accum_out=col(2, i % 2, 2)[:, a:a + 1])
                        e.then_inc(m_p, 1)
                    if i >= 1:
                        k = i - 1
                        act.wait_ge(m_t, p * SB + k + 1)
                        act.wait_ge(m_o, max(0, p * SB + k - 1))
                        nc.scalar.activation(ring[:, 2 + k % 2, :], ps[:, 4 + k % 2, :], ACT.Copy).then_inc(m_pt, 1)
                    if 4 <= i < 4 + DC:
                        split_hi(C_M + p + 1, NARROW, i - 4, (m_pj, (p + 1) * NT))

            def df_place_hi(h, n, part):
                cols = slice(n % NT * TQ, (n % NT + 1) * TQ)
                if part == 0:
                    if n >= 2:
                        act.wait_ge(df_pl_d, h * 16 + 4 * (n - 1))
                        act.wait_ge(df_lo, h * NT + (n - 1))
                    act.wait_ge(df_x2, h * NT + (n + 1))
                    nc.scalar.activation(hi_tmp[:, n % 2, :], ring[:, XR_SLOT, :], ACT.Copy).then_inc(df_hi, 1)
                if part in (1, 2):
                    m = part - 1
                    if m == 0:
                        act.wait_ge(df_hi, h * NT + (n + 1))
                    for r in (0, 2 * DQ):
                        k0 = 2 * DQ + m * DQ
                        nc.scalar.activation(df_s[m][r:r + DQ, cols], hi_tmp[k0:k0 + DQ, n % 2, :].bitcast(F32), ACT.Copy).then_inc(df_pl_a, 1)

            def df_exp(h, i):
                j0 = DF_STEPS[i][2]
                act.wait_ge(df_o, 1 + h * N_DF + max(0, i - 2))
                act.wait_ge(df_z, h * N_DF + (i + 1))
                nc.scalar.activation(ring[:, i % 3, j0 * P:], ps[:, i % 2, j0 * P:], ACT.Exp, scale=DQ ** -0.5).then_inc(df_e, 1)

            def df_move(h, n):
                if n >= 1:
                    act.wait_ge(df_t1, 1 + h * NT + n)
                    act.wait_ge(df_px, h * NT + n)
                act.wait_ge(df_pj, h * NT + (n + 1))
                nc.scalar.activation(ring[:, X_SLOT, :], ps[:, PJ_BANK[n], :], ACT.Copy).then_inc(df_x, 1)

            def differential(h, order, final=False):
                for what, k in order:
                    if what == "s":
                        df_exp(h, k)
                        if not final and DF_SPLIT <= k < DF_SPLIT + DC:
                            split_hi(h + (C_DF + 1), NARROW, k - DF_SPLIT, (df_pj, h * NT + NT))
                    if what == "x":
                        df_move(h, k)
                    if what == "R":
                        df_place_hi(h, *k)
                    if what == "l":
                        rsqrt_of(col(4, 0, 4), col(5, 0, 4), col(6, 0, 4), df_var, h * NT + (k + 1), df_ln, df_y0)
                    if what == "w":
                        act.wait_ge(wo_in[k % 2], 16 * (k // 2 + 1))
                        nc.scalar.activation(wo_hi[:, k, :], w_raw[:, (k % 2) * D:(k % 2 + 1) * D], ACT.Copy).then_inc(wo_hi_ok, 1)

            differential(0, DF_START)
            with act.Fori(0, DF_H - 1) as h:
                differential(h, DF_ORDER[False])
            differential(DF_H - 1, DF_ORDER[True], True)

            def out_hi(t, u, free):
                act.wait_ge(o_tps, t + 1)
                if free is not None:
                    act.wait_ge(o_ps, free)
                for g in range(2):
                    nc.scalar.activation(yt_hi[:, u, 4 * g:4 * g + 4, :],
                                         ps[:, 2 * u + g, :].rearrange("p (c s) -> p c s", c=4), ACT.Copy).then_inc(o_thi, 1)

            def out_square(t, u, free):
                if free is not None:
                    act.wait_ge(o_out[u], free)
                    act.wait_ge(o_fin, t - 1)
                for g in range(2):
                    act.wait_ge(o_ps, t * 2 + (g + 1))
                    nc.scalar.activation(ob[:, u, g * 512:(g + 1) * 512], ps[:, 4 + 2 * u + g, :], ACT.Square,
                                         accum_out=col(g, u)).then_inc(o_sq, 1)
                rsqrt_of(col(2, u), col(3, u), col(4, u), o_var, t + 1, o_ln, o_y0)

            out_hi(0, 0, None)
            out_hi(1, 1, None)
            out_square(0, 0, None)
            out_hi(2, 0, 2)
            out_square(1, 1, None)
            with act.Fori(0, SB // 2 - 2) as i:
                for u in range(2):
                    out_hi(i * 2 + (u + 3), 1 - u, i * 4 + (2 * u + 4))
                    out_square(i * 2 + (u + 2), u, i * 16 + 16)
            out_hi(SB - 1, 1, 2 * (SB - 2))
            out_square(SB - 2, 0, 16 * (SB // 2 - 1))
            out_square(SB - 1, 1, 16 * (SB // 2 - 1))

        @block.vector
        def _(dve):
            def split_lo(c, cols, dc):
                dve.wait_ge(w_hi_ok, c * DC + (dc + 1))
                nc.vector.tensor_tensor(w_lo(cols, dc), raw(cols, dc), w_hi(cols, dc).bitcast(F32), ALU.subtract).then_inc(w_lo_ok, 1)

            def newton(var, y0, tmp, y, chain, n):
                nc.vector.tensor_tensor(tmp, y0, y0, ALU.mult).then_inc(chain, 1)
                dve.wait_ge(chain, n + 1)
                nc.vector.tensor_tensor(tmp, tmp, var, ALU.mult).then_inc(chain, 1)
                dve.wait_ge(chain, n + 2)
                nc.vector.tensor_scalar(tmp, tmp, -0.5, 1.5, ALU.mult, ALU.add).then_inc(chain, 1)
                dve.wait_ge(chain, n + 3)
                nc.vector.tensor_tensor(y, tmp, y0, ALU.mult).then_inc(chain, 1)
                dve.wait_ge(chain, n + 4)

            dve.wait_ge(const_in, 80)
            for k, dst in enumerate((ident, negtri, rotperm, ident_b, sb_mask, df_mask_kq, df_mask_qk, ident_r)):
                src = (0, 1, 2, 0, 3, 4, 5, 0)[k]
                nc.vector.tensor_copy(dst[:], cst[:, src, :]).then_inc(const_ok, 1)
            nc.vector.memset(v1[:, :, HD:HD + 1], 1.0).then_inc(lam_ch, 1)
            lam4 = lam_in.rearrange("p (a b d) -> p a b d", a=2, b=2)
            prod = ring[:, 0, 0:2 * DQ].rearrange("p (a d) -> p a d", a=2)
            nc.vector.tensor_tensor(prod, lam4[:, :, 0, :], lam4[:, :, 1, :], ALU.mult).then_inc(sb_ch, 1)
            dve.wait_ge(sb_ch, 1)
            nc.vector.tensor_reduce(small[:, 4:6], prod, AXX, ALU.add).then_inc(lam_ch, 1)
            nc.vector.tensor_scalar(gsub_b, gsub_b, 1.0 - LAMBDA_INIT, None, ALU.mult).then_inc(sb_ch, 1)

            def norm_var(t, u):
                dve.wait_ge(x_sq, t + 1)
                nc.vector.tensor_scalar(col(1, u), col(0, u), 1.0 / D, EPS, ALU.mult, ALU.add).then_inc(x_var, 1)

            def norm_rows(t, u):
                dve.wait_ge(x_y0, t + 1)
                newton(col(1, u), col(3, u), col(4, u), col(5, u), x_nr, t * 4)
                nc.vector.scalar_tensor_tensor(out=hb[:, u, :], in0=xb[:, u, :], scalar=col(5, u), in1=gpre_b[:],
                                               op0=ALU.mult, op1=ALU.mult).then_inc(h_rows, 1)

            def norm_lo(t, u):
                for g in range(2):
                    dve.wait_ge(ht_hi_ok, t * 2 + (g + 1))
                    rows = (slice(None), slice(4 * g, 4 * g + 4), bass.ts(t, P))
                    nc.vector.tensor_tensor(ht_lo[rows], ps[:, 2 * u + g, :].rearrange("p (c s) -> p c s", c=4),
                                            ht_hi[rows].bitcast(F32), ALU.subtract).then_inc(ht_lo_ok, 1)

            norm_var(0, 0)
            norm_rows(0, 0)
            dve.wait_ge(lam_e, 1)
            nc.vector.tensor_tensor(small[:, 6:7], small[:, 2:3], small[:, 3:4], ALU.subtract).then_inc(sb_ch, 1)
            dve.wait_ge(sb_ch, 3)
            nc.vector.tensor_scalar(lam, small[:, 6:7], LAMBDA_INIT, None, ALU.add).then_inc(sb_ch, 1)
            for dc in range(DC):
                split_lo(0, WIDE, dc)
            with dve.Fori(0, SB // 2 - 1) as i:
                for q in range(2):
                    norm_var(i * 2 + (q + 1), 1 - q)
                    norm_lo(i * 2 + q, q)
                    norm_rows(i * 2 + (q + 1), 1 - q)
            norm_var(SB - 1, 1)
            norm_lo(SB - 2, 0)
            norm_rows(SB - 1, 1)
            norm_lo(SB - 1, 1)

            two_pi = 2 * math.pi
            c1 = 201 / 32
            c2 = round((two_pi - c1) * 2 ** 21) / 2 ** 21
            c3 = two_pi - c1 - c2
            magic = 1.5 * 2 ** 23
            pi_in = 3.1415925
            dve.wait_ge(pos_in, 16)
            nc.vector.tensor_scalar(ang[:], red[:].bitcast(I32), invf, None, ALU.mult).then_inc(trig_ch, 1)
            dve.wait_ge(trig_ch, 1)
            nc.vector.tensor_scalar(turns[:], ang[:], 1 / two_pi, magic, ALU.mult, ALU.add).then_inc(trig_ch, 1)
            dve.wait_ge(trig_ch, 2)
            nc.vector.tensor_scalar(turns[:], turns[:], magic, None, ALU.subtract).then_inc(trig_ch, 1)
            dve.wait_ge(trig_ch, 3)
            for k, (part, base) in enumerate(((c1, ang), (c2, red), (c3, red))):
                nc.vector.scalar_tensor_tensor(out=red[:], in0=turns[:], scalar=-part, in1=base[:],
                                               op0=ALU.mult, op1=ALU.add).then_inc(trig_ch, 1)
                dve.wait_ge(trig_ch, 4 + k)
            nc.vector.tensor_scalar(turns[:], red[:], math.pi / 2, -two_pi, ALU.is_gt, ALU.mult).then_inc(trig_ch, 1)
            dve.wait_ge(trig_ch, 7)
            nc.vector.scalar_tensor_tensor(out=ang[:], in0=red[:], scalar=math.pi / 2, in1=turns[:],
                                           op0=ALU.add, op1=ALU.add).then_inc(trig_ch, 1)
            dve.wait_ge(trig_ch, 8)
            nc.vector.tensor_scalar(red[:], red[:], pi_in, -pi_in, ALU.min, ALU.max).then_inc(trig_ch, 1)
            nc.vector.tensor_scalar(ang[:], ang[:], pi_in, -pi_in, ALU.min, ALU.max).then_inc(trig_ch, 1)

            with dve.Fori(0, N_V) as c:
                for dc in range(DC):
                    split_lo(c + 1, WIDE, dc)

            def gates(c, cols):
                for b in range(8):
                    if b == 7:
                        for dc in range(DC):
                            split_lo(c + (N_V + 1), cols, dc)
                    e = ring[:, 2 + b % 2, :]
                    dve.wait_ge(vg_e, c * 8 + (b + 1))
                    nc.vector.tensor_scalar(e, e, 1.0, None, ALU.add).then_inc(vg_ch, 1)
                    dve.wait_ge(vg_ch, c * 16 + (2 * b + 1))
                    nc.vector.reciprocal(e, e).then_inc(vg_ch, 1)
                    dve.wait_ge(vg_out[b % 2], 1 + c * 128 + (128 * N_V + 32 * (b // 2)))
                    dve.wait_ge(vg_ch, c * 16 + (2 * b + 2))
                    nc.vector.tensor_tensor(ring[:, b % 2, :], ps[:, b, :], e, ALU.mult).then_inc(vg_ok, 1)

            with dve.Fori(0, N_G - 1) as c:
                gates(c, WIDE)
            gates(N_G - 1, NARROW)

            def sb_softplus(h, i):
                j0 = SB_STEPS[i % N_ST][2]
                dve.wait_ge(sb_ln, h * N_ST + (i + 1))
                sp_ = ring[:, i % 4, j0 * P:]
                nc.vector.scalar_tensor_tensor(out=sp_, in0=sp_, scalar=Z_MAX, in1=ps[:, Z_BANK[i % 5], j0 * P:],
                                               op0=ALU.min, op1=ALU.max).then_inc(sb_sp, 1)
                dve.wait_ge(sb_sp, h * N_ST + (i + 1))
                nc.vector.tensor_copy(sp_hi[:, i % 4, j0 * P:], sp_).then_inc(sb_hi, 1)

            def sb_add(h, i):
                t, kb, j0 = SB_STEPS[i]
                o = ps[:, 4 + i % 2, 0:4 * (HD + 1)].rearrange("p (j d) -> p j d", j=4)[:, j0:, :]
                a = acc[:, t % 2, j0:, :]
                dve.wait_ge(sb_o, 1 + h * N_ST + (i + 1))
                if kb == 0:
                    dve.wait_ge(sb_yout[t % 2], 1 + h * 32 + (16 if t >= 2 else 0))
                    nc.vector.tensor_copy(a, o[:, :, 0:HD]).then_inc(sb_acc, 1)
                    return
                dve.wait_ge(sb_acc, 1 + h * N_ST + i)
                nc.vector.scalar_tensor_tensor(out=a, in0=o[:, :, HD:HD + 1].broadcast_to((P, 4 - j0, HD)), scalar=-1.0, in1=a,
                                               op0=ALU.add, op1=ALU.mult).then_inc(sb_ch, 1)
                dve.wait_ge(sb_ch, h * len(SB_MULS) + (5 + SB_MULS.index(i)))
                nc.vector.tensor_tensor(a, o[:, :, 0:HD], a, ALU.subtract).then_inc(sb_acc, 1)

            def sb_stack_lo(h, n, k):
                cols = slice(n % NT * TQ, (n % NT + 1) * TQ)
                dve.wait_ge(sp_act, h * 12 + (3 * n + 3))
                if k == 0:
                    nc.vector.scalar_tensor_tensor(out=sb_mb[HD:P, cols], in0=ps[0:HD, 7, :], scalar=HD ** -0.5,
                                                   in1=sb_ma[0:HD, cols].bitcast(F32), op0=ALU.mult, op1=ALU.subtract).then_inc(sp_dve, 1)
                if k == 1:
                    nc.vector.tensor_tensor(sb_s[0:HD, cols], ps[HD:P, 7, :], sb_s[HD:P, cols].bitcast(F32),
                                            ALU.subtract).then_inc(sp_dve, 1)

            def sb_slot(h, i, more):
                if i >= 5:
                    sb_add(h, i - 5)
                if 1 <= i and (more or i <= N_ST):
                    sb_softplus(h, i - 1)
                for ahead, n, at in SB_PROJECT:
                    if at + 5 <= i < at + 7 and (more or not ahead):
                        sb_stack_lo(h, ahead * NT + n, i - at - 5)
                if SB_SPLIT < i <= SB_SPLIT + DC:
                    split_lo(h + (C_SB + 1), NARROW, i - SB_SPLIT - 1)

            dve.wait_ge(trig_out, 32)
            nc.vector.memset(sb_mb[0:HD, :].bitcast(F32), 0.0).then_inc(sb_zero, 1)
            for n in range(2):
                for k in range(2):
                    sb_stack_lo(0, n, k)
            for i in range(SB_LEAD):
                sb_slot(0, i, True)
            with dve.Fori(0, SB_H - 1) as h:
                for i in range(SB_LEAD, SB_LEAD + N_ST):
                    sb_slot(h, i, True)
            for i in range(SB_LEAD, SB_LEAD + N_ST):
                sb_slot(SB_H - 1, i, False)

            for b in range(2):
                dve.wait_ge(mm_sq, b + 1)
                nc.vector.tensor_scalar(col(1, b), col(0, b), 1.0 / D, EPS, ALU.mult, ALU.add).then_inc(mm_ch, 1)
                dve.wait_ge(mm_y0, b + 1)
                newton(col(1, b), col(3, b), col(4, b), col(5, b), mm_ch, 5 * b + 1)
                nc.vector.scalar_tensor_tensor(out=mem_h, in0=mem_x, scalar=col(5, b), in1=mem_g,
                                               op0=ALU.mult, op1=ALU.mult).then_inc(mm_h, 1)
                for g in range(2):
                    dve.wait_ge(mm_hi, 2 * b + g + 1)
                    rows = (slice(None), slice(4 * g, 4 * g + 4), slice(b * P, (b + 1) * P))
                    nc.vector.tensor_tensor(mt_lo[rows], ps[:, g, :].rearrange("p (c s) -> p c s", c=4),
                                            mt_hi[rows].bitcast(F32), ALU.subtract).then_inc(mm_lo, 1)
            for k in range(4):
                for dc in range(DC):
                    split_lo(C_MK + k + 1, NARROW, dc)
                if k < 2:
                    dve.wait_ge(mm_ka, k + 1)
                    nc.vector.tensor_tensor(km_lo[:, k, :], ps[:, 2 + k, 0:NMEM], km_hi[:, k, :].bitcast(F32), ALU.subtract).then_inc(mm_kd, 1)

            for p in range(2):
                for n in range(NT):
                    cols = slice(n * TQ, (n + 1) * TQ)
                    dve.wait_ge(m_qhi, p * NT + n + 1)
                    nc.vector.scalar_tensor_tensor(out=qm_lo[:, cols], in0=ps[:, 6 + n % 2, :], scalar=HD ** -0.5,
                                                   in1=qm_hi[:, cols].bitcast(F32), op0=ALU.mult, op1=ALU.subtract).then_inc(m_qlo, 1)
                for i in range(SB + 2):
                    if i < SB:
                        dve.wait_ge(m_s, p * SB + i + 1)
                        nc.vector.tensor_reduce(col(0, i % 2, 2), ps[:, 2 * (i % 2):2 * (i % 2) + 2, 0:NMEM], AXX, ALU.max).then_inc(m_mx, 1)
                        dve.wait_ge(m_mx, p * SB + i + 1)
                        dve.wait_ge(m_p, max(0, p * SB + i - 1))
                        nc.vector.tensor_scalar(col(1, i % 2, 2), col(0, i % 2, 2), -1.0, None, ALU.mult).then_inc(m_nm, 1)
                    if i >= 2:
                        k = i - 2
                        dve.wait_ge(m_o, p * SB + k + 1)
                        dve.wait_ge(m_yout[k % 2], 16 * (p * SB // 2 + k // 2))
                        nc.vector.reciprocal(col(3, k % 2, 2), col(2, k % 2, 2)).then_inc(m_rc, 1)
                        dve.wait_ge(m_rc, p * SB + k + 1)
                        nc.vector.tensor_tensor(acc[:, k % 2, 0:2, :], ps[:, 6 + k % 2, 0:2 * HD].rearrange("p (a d) -> p a d", a=2),
                                                col(3, k % 2, 2).unsqueeze(2).broadcast_to((P, 2, HD)), ALU.mult).then_inc(m_y, 1)
                    if 5 <= i < 5 + DC:
                        split_lo(C_M + p + 1, NARROW, i - 5)

            pmax = small[:, 128:160].rearrange("p (m j c) -> p m j c", m=2, j=4)
            mx8 = small[:, 160:168]
            rc = small[:, 168:176].rearrange("p (m j) -> p m j", m=2)
            second = ring[:, 3, 0:256].rearrange("p (j d) -> p j d", j=4)
            square = ring[:, 3, 256:512].rearrange("p (j d) -> p j d", j=4)

            def df_rotate(h, n, part):
                cols = slice(n % NT * TQ, (n % NT + 1) * TQ)
                x2 = ring[:, XR_SLOT, :]
                if part == 0:
                    dve.wait_ge(df_px, h * NT + (n + 1))
                    if n >= 1:
                        dve.wait_ge(df_hi, h * NT + n)
                        dve.wait_ge(df_lo, h * NT + n)
                    nc.vector.tensor_tensor(x2, ps[:, EX_BANK[n], :], sin_c, ALU.mult).then_inc(df_t2, 1)
                    dve.wait_ge(df_t2, 1 + h * NT + (n + 1))
                    dve.wait_ge(df_t1, 1 + h * NT + (n + 1))
                    nc.vector.tensor_tensor(x2, x2, ring[:, XC_SLOT, :], ALU.add).then_inc(df_x2, 1)
                if part == 1:
                    dve.wait_ge(df_hi, h * NT + (n + 1))
                    if n >= 2:
                        dve.wait_ge(df_pl_p, 1 + h * 24 + 6 * (n - 1))
                    nc.vector.tensor_tensor(lo_tmp[:, n % 2, :], x2, hi_tmp[:, n % 2, :].bitcast(F32), ALU.subtract).then_inc(df_lo, 1)
                if part >= 2:
                    m = part - 2
                    for r in (0, DQ):
                        nc.vector.tensor_copy(df_m[m][r:r + DQ, cols], hi_tmp[m * DQ:(m + 1) * DQ, n % 2, :].bitcast(F32)).then_inc(df_pl_d, 1)

            def df_unit(h, u):
                kind, t, j, m, c, w = DF_UNITS[u]
                dve.wait_ge(df_ups, h * N_UN + (u + 1))
                if kind == "row":
                    nc.vector.tensor_copy(df_m[m][96:97, t * TQ:(t + 1) * TQ], ps[96:97, 2 + u % 2, :]).then_inc(df_mx, 1)
                    return
                nc.vector.tensor_reduce(pmax[:, m, j, c:c + 1], ps[:, 2 + u % 2, 0:w], AXX, ALU.max).then_inc(df_mx, 1)
                if DF_UNITS[u + 1][0] == "row":
                    dve.wait_ge(df_mx, 1 + h * N_UN + (u + 1))
                    nc.vector.tensor_reduce(mx8, pmax.rearrange("p m j c -> p (m j) c")[:, :, 0:t + 1], AXX, ALU.max).then_inc(df_cb, 1)
                    dve.wait_ge(df_cb, h * NT + (t + 1))
                    nc.vector.tensor_scalar(nm_win[:, 96:104], mx8, -1.0, None, ALU.mult).then_inc(df_nm, 1)

            def df_end(h, t):
                o = [ps[:, 4 + 2 * (t % 2) + m, 0:4 * (HD + 1)].rearrange("p (j d) -> p j d", j=4) for m in range(2)]
                a, ch = acc[:, t % 2], h * 24 + 6 * t
                dve.wait_ge(df_o, 1 + h * N_DF + (max(i for i, s in enumerate(DF_STEPS) if s[0] == t) + 1))
                dve.wait_ge(df_yout[t % 2], 1 + h * 32 + (16 if t >= 2 else 0))
                for m in range(2):
                    nc.vector.reciprocal(rc[:, m, :], o[m][:, :, HD]).then_inc(df_fch, 1)
                dve.wait_ge(df_fch, ch + 2)
                nc.vector.tensor_scalar(rc[:, 1, :], rc[:, 1, :], lam, None, ALU.mult).then_inc(df_fch, 1)
                nc.vector.tensor_tensor(a, o[0][:, :, 0:HD], rc[:, 0, :].unsqueeze(2).broadcast_to((P, 4, HD)), ALU.mult).then_inc(df_fch, 1)
                dve.wait_ge(df_fch, ch + 4)
                nc.vector.tensor_tensor(second, o[1][:, :, 0:HD], rc[:, 1, :].unsqueeze(2).broadcast_to((P, 4, HD)), ALU.mult).then_inc(df_fin, 1)
                dve.wait_ge(df_fin, 1 + h * NT + (t + 1))
                nc.vector.tensor_tensor(a, a, second, ALU.subtract).then_inc(df_fch, 1)
                dve.wait_ge(df_fch, ch + 5)
                nc.vector.tensor_tensor(square, a, a, ALU.mult).then_inc(df_fch, 1)
                dve.wait_ge(df_fch, ch + 6)
                nc.vector.tensor_reduce(col(3, 0, 4), square, AXX, ALU.add).then_inc(df_gch, 1)
                dve.wait_ge(df_gch, h * 24 + (6 * t + 1))
                nc.vector.tensor_scalar(col(4, 0, 4), col(3, 0, 4), 1.0 / HD, EPS, ALU.mult, ALU.add).then_inc(df_var, 1)

            def df_norm(h, t):
                a = acc[:, t % 2]
                dve.wait_ge(df_y0, h * NT + (t + 1))
                newton(col(4, 0, 4), col(6, 0, 4), col(5, 1, 4), col(6, 1, 4), df_gch, h * 24 + (6 * t + 1))
                nc.vector.tensor_tensor(a, a, col(6, 1, 4).unsqueeze(2).broadcast_to((P, 4, HD)), ALU.mult).then_inc(df_gch, 1)
                dve.wait_ge(df_gch, h * 24 + (6 * t + 6))
                nc.vector.tensor_tensor(a, a, gsub_b.unsqueeze(1).broadcast_to((P, 4, HD)), ALU.mult).then_inc(df_yok, 1)

            def df_cosine(h, n):
                dve.wait_ge(df_x, h * NT + (n + 1))
                dve.wait_ge(df_cs, h * 128 + 32 * (n + 1))
                if n >= 2:
                    dve.wait_ge(df_x2, h * NT + n)
                nc.vector.tensor_tensor(ring[:, XC_SLOT, :], ring[:, X_SLOT, :], cos_c, ALU.mult).then_inc(df_t1, 1)

            def differential(h, order, final=False):
                for what, k in order:
                    if what == "u":
                        df_unit(h, k)
                    if what == "s" and not final and DF_SPLIT < k <= DF_SPLIT + DC:
                        split_lo(h + (C_DF + 1), NARROW, k - DF_SPLIT - 1)
                    if what == "r":
                        df_cosine(h, k)
                    if what == "R":
                        df_rotate(h, *k)
                    if what == "f":
                        df_end(h, k)
                    if what == "g":
                        df_norm(h, k)
                    if what == "w":
                        dve.wait_ge(wo_hi_ok, k + 1)
                        nc.vector.tensor_tensor(wo_lo[:, k, :], w_raw[:, (k % 2) * D:(k % 2 + 1) * D], wo_hi[:, k, :].bitcast(F32),
                                                ALU.subtract).then_inc(wo_lo_ok, 1)

            nc.vector.memset(nm_win[:].bitcast(F32), 0.0).then_inc(df_win, 1)
            dve.wait_ge(df_win, 1)
            dve.wait_ge(df_set, 6)
            differential(0, DF_START)
            with dve.Fori(0, DF_H - 1) as h:
                differential(h, DF_ORDER[False])
            differential(DF_H - 1, DF_ORDER[True], True)

            def out_gate(t, u, value):
                dve.wait_ge(o_in[u], value)
                nc.vector.tensor_tensor(yb[:, u, :], yb[:, u, :], gb[:, u, :], ALU.mult).then_inc(o_yg, 1)

            def out_lo(t, u):
                for g in range(2):
                    dve.wait_ge(o_thi, t * 2 + (g + 1))
                    nc.vector.tensor_tensor(yt_lo[:, u, 4 * g:4 * g + 4, :], ps[:, 2 * u + g, :].rearrange("p (c s) -> p c s", c=4),
                                            yt_hi[:, u, 4 * g:4 * g + 4, :].bitcast(F32), ALU.subtract).then_inc(o_tlo, 1)

            def out_norm(t, u, value):
                dve.wait_ge(o_sq, t * 2 + 2)
                nc.vector.tensor_tensor(col(5, u), col(0, u), col(1, u), ALU.add).then_inc(o_ch, 1)
                dve.wait_ge(o_ch, t + 1)
                nc.vector.tensor_scalar(col(2, u), col(5, u), 1.0 / D, EPS, ALU.mult, ALU.add).then_inc(o_var, 1)
                dve.wait_ge(o_y0, t + 1)
                newton(col(2, u), col(4, u), col(5, u), small[:, 4 + u:5 + u], o_nr, t * 4)
                for g in range(2):
                    cols = slice(g * 512, (g + 1) * 512)
                    nc.vector.scalar_tensor_tensor(out=ob[:, u, cols], in0=ps[:, 4 + 2 * u + g, :], scalar=small[:, 4 + u:5 + u],
                                                   in1=gpost_b[:, cols], op0=ALU.mult, op1=ALU.mult).then_inc(o_n, 1)
                dve.wait_ge(o_n, t * 2 + 2)
                dve.wait_ge(o_xr[u], value)
                nc.vector.tensor_tensor(ob[:, u, :], ob[:, u, :], xr[:, u, :], ALU.add).then_inc(o_fin, 1)

            dve.wait_ge(gpost_in, 16)
            out_gate(0, 0, 32)
            out_gate(1, 1, 32)
            out_lo(0, 0)
            out_lo(1, 1)
            out_gate(2, 0, 64)
            out_norm(0, 0, 16)
            out_lo(2, 0)
            out_gate(3, 1, 64)
            out_norm(1, 1, 16)
            with dve.Fori(0, SB // 2 - 2) as i:
                for u in range(2):
                    out_lo(i * 2 + (u + 3), 1 - u)
                    out_gate(i * 2 + (u + 4), u, i * 32 + 96)
                    out_norm(i * 2 + (u + 2), u, i * 16 + 32)
            out_lo(SB - 1, 1)
            out_norm(SB - 2, 0, 16 * SB // 2)
            out_norm(SB - 1, 1, 16 * SB // 2)

        @block.gpsimd
        def _(pool):
            with pool.Fori(0, SB_H) as h:
                for i in range(N_ST):
                    j0 = SB_STEPS[i % N_ST][2]
                    pool.wait_ge(sb_hi, h * N_ST + (i + 1))
                    pool.sem_inc(pool_go, 1)
                    nc.gpsimd.tensor_tensor(ring_r[:, i % 4, j0 * P:], ring[:, i % 4, j0 * P:],
                                            sp_hi[:, i % 4, j0 * P:].bitcast(F32), ALU.subtract).then_inc(sb_lo, 1)

            pool.wait_ge(m_y, 2 * SB)
            for m in range(2):
                for dst in (df_s, df_m):
                    nc.gpsimd.memset(dst[m][96:P, :].bitcast(F32), 0.0).then_inc(df_set, 1)
            pool.wait_ge(df_set, 4)
            for m in range(2):
                nc.gpsimd.memset(df_s[m][96:97, :].bitcast(F32), 1.0).then_inc(df_set, 1)

            def differential(h):
                for n in range(NT):
                    cols = slice(n * TQ, (n + 1) * TQ)
                    pool.wait_ge(df_lo, h * NT + (n + 1))
                    for m in range(2):
                        pool.wait_ge(df_pl_p, 1 + h * 24 + (6 * n + m))
                        pool.sem_inc(pool_go, 1)
                        nc.gpsimd.memset(df_m[m][96:97, cols].bitcast(F32), 0.0).then_inc(df_pl_p, 1)
                    for m in range(2):
                        for k, (dst, q0, src) in enumerate(((df_s, DQ, 2 * DQ + m * DQ), (df_m, 2 * DQ, m * DQ))):
                            pool.wait_ge(df_pl_p, 1 + h * 24 + (6 * n + 2 + 2 * m + k))
                            pool.sem_inc(pool_go, 1)
                            nc.gpsimd.tensor_scalar(dst[m][q0:q0 + DQ, cols], lo_tmp[src:src + DQ, n % 2, :].bitcast(F32),
                                                    1.0, 0.0, ALU.mult, ALU.add).then_inc(df_pl_p, 1)

            with pool.Fori(0, DF_H) as h:
                differential(h)

            pool.wait_ge(df_t2, 1 + DF_H * NT)
            pool.wait_ge(w_lo_ok, (C_DF + DF_H) * DC)
            for dc in range(DC):
                if dc >= 2:
                    pool.wait_ge(wo_lo_ok, dc - 1)
                nc.gpsimd.dma_start(w_raw[:, (dc % 2) * D:(dc % 2 + 1) * D], w_out[dc * P:(dc + 1) * P, :]).then_inc(wo_in[dc % 2], 16)


def kernel(x, mem, positions, w_in, w_mem_kv, w_out, g_pre, g_post, g_mem, g_subln, df_lambda):
    import concourse.bacc as bacc
    from concourse.bass_utils import run_bass_kernel_spmd

    def tiled(cols):
        return np.ascontiguousarray(cols.reshape(DC, P, -1).transpose(1, 0, 2).reshape(P, -1))

    w = np.asarray(w_in)[0]
    names = ("sb_q", "sb_k", "sb_v", "sb_g", "df_q", "df_k", "df_v", "df_g", "m_q", "m_g")
    sizes = (512, 512, 512, 512, 256, 256, 256, 256, 256, 256)
    part, at = {}, 0
    for name, n in zip(names, sizes):
        part[name] = w[:, at:at + n]
        at += n
    wide = np.concatenate([part[n] for n in ("sb_v", "df_v", "sb_g", "df_g", "m_g")], axis=1)
    wide = np.stack([tiled(wide[:, c * WIDE:(c + 1) * WIDE]) for c in range(N_V + N_G)])
    kv = np.asarray(w_mem_kv)[0]

    def head(q, k, h):
        return np.concatenate([part[q][:, h * HD:(h + 1) * HD], part[k][:, h * HD:(h + 1) * HD]], axis=1)

    narrow = [head("sb_q", "sb_k", h) for h in range(SB_H)]
    narrow += [kv[:, c * P:(c + 1) * P] for c in range(4)]
    narrow += [part["m_q"][:, c * P:(c + 1) * P] for c in range(2)]
    narrow += [head("df_q", "df_k", h) for h in range(DF_H)]
    narrow = np.stack([tiled(c) for c in narrow])

    r = np.arange(P)
    rot = np.zeros((P, P), np.float32)
    for g in range(0, P, DQ):
        for j in range(4):
            rot[g + 4 + j, g + j] = -1.0
            rot[g + j, g + 4 + j] = 1.0
    late = (r[:, None] >= 64) & (r[None, :] < 64)
    const_sq = np.stack([
        np.eye(P), -(r[:, None] >= r[None, :]).astype(np.float32), rot,
        NEG * (r[:, None] >= r[None, :]), NEG * late, NEG * late.T]).astype(np.float32)
    inv = np.float32(1.0) / (np.float32(THETA) ** (np.arange(0, 8, 2, dtype=np.float32) / np.float32(8)))
    const_col = np.zeros((P, 1), np.float32)
    for g in range(0, P, DQ):
        const_col[g:g + 4, 0] = inv
        const_col[g + 4:g + 8, 0] = inv

    arrays = {
        "x": np.asarray(x)[0], "mem": np.asarray(mem)[0], "positions": np.asarray(positions),
        "w_wide": wide, "w_narrow": narrow, "w_out": np.asarray(w_out)[0],
        "g_pre": np.asarray(g_pre), "g_post": np.asarray(g_post), "g_mem": np.asarray(g_mem),
        "g_subln": np.asarray(g_subln), "df_lambda": np.asarray(df_lambda).reshape(1, 4 * DQ),
        "const_sq": const_sq, "const_col": const_col,
    }
    nc = bacc.Bacc("TRN2", target_bir_lowering=False, num_devices=1)
    arrays = {f"in_{n}": np.ascontiguousarray(a) for n, a in arrays.items()}
    args = [nc.dram_tensor(n, a.shape, mybir.dt.from_np(a.dtype), kind="ExternalInput").ap() for n, a in arrays.items()]
    args.append(nc.dram_tensor("out_y", (S, D), F32, kind="ExternalOutput").ap())
    build(nc, *args)
    r = run_bass_kernel_spmd(nc, [arrays], core_ids=[0])
    return r.results[0]["out_y"].reshape(1, S, D)
```
